# Optimizing a Trainium2 kernel written in Bass

```python
import jax, jax.numpy as jnp
from jax import lax
import numpy as np

D_MODEL = 1024
BATCH = 1
SEQ = 256
DEPTH = 1
DEC_BATCH = 8
DEC_SEQ = 1
PAST_LEN = 1024
PAGE_SIZE = 128

SSM_EXPAND = 2
D_INNER = SSM_EXPAND * D_MODEL
SSM_HEAD_DIM = 64
SSM_HEADS = D_INNER // SSM_HEAD_DIM
SSM_GROUPS = 4
SSM_HEADS_PER_GROUP = SSM_HEADS // SSM_GROUPS
D_STATE = 128
CONV_WIDTH = 4
CONV_DIM = D_INNER + 2 * SSM_GROUPS * D_STATE
SSD_CHUNK = 128
ATTN_HEAD_DIM = 64
HEADS_PER_DIL_GROUP = 4
DIL_GROUPS = ((128, 1), (512, 4), (2048, 16))
N_ATTN_HEADS = HEADS_PER_DIL_GROUP * len(DIL_GROUPS)
ATTN_WIDTH = N_ATTN_HEADS * ATTN_HEAD_DIM
ATTN_OUT_WIDTH = HEADS_PER_DIL_GROUP * ATTN_HEAD_DIM
PROJ_SIZES = (D_INNER, CONV_DIM, SSM_HEADS, ATTN_WIDTH, ATTN_WIDTH, ATTN_WIDTH, D_MODEL, D_MODEL)
D_IN_PROJ = D_INNER + CONV_DIM + SSM_HEADS + 3 * ATTN_WIDTH + 2 * D_MODEL
N_EXPERTS = 32
TOP_K = 4
D_FF = D_MODEL
SWIGLU_LIMIT = 7.0
SWIGLU_ALPHA = 1.702
MOE_BLOCK = 128
ALPHA = (2.0 * DEPTH) ** 0.25
BETA = (8.0 * DEPTH) ** -0.25
NORM_EPS = 1e-5

kernel_name = "hybrid_ssd_dilated_alibi_moe_decode_step"

def layer_norm(x, g, b):
    xf = x.astype(jnp.float32)
    mu = jnp.mean(xf, axis=-1, keepdims=True)
    var = jnp.mean(jnp.square(xf - mu), axis=-1, keepdims=True)
    return ((xf - mu) * lax.rsqrt(var + NORM_EPS) * g + b).astype(x.dtype)

def group_rms_norm(y, g):
    shp = y.shape
    yg = y.reshape(shp[:-1] + (SSM_GROUPS, D_INNER // SSM_GROUPS))
    yg = yg * lax.rsqrt(jnp.mean(jnp.square(yg), axis=-1, keepdims=True) + NORM_EPS)
    return yg.reshape(shp) * g

def alibi_slopes():
    return jnp.asarray(2.0 ** (-8.0 * np.arange(1, N_ATTN_HEADS + 1) / N_ATTN_HEADS), dtype=jnp.float32)

def causal_dwconv(x_ext, w, b):
    y = lax.conv_general_dilated(x_ext, w[:, None, :].astype(x_ext.dtype), window_strides=(1,), padding='VALID',
                                 dimension_numbers=('NWC', 'WIO', 'NWC'), feature_group_count=CONV_DIM)
    return y + b

def ssd_scan(xs, dt, A, Bm, Cm, h0):
    f32 = jnp.float32
    Bsz, T = xs.shape[0], xs.shape[1]
    lc = min(SSD_CHUNK, T)
    nc = -(-T // lc)
    pad = nc * lc - T
    padt = lambda t: jnp.pad(t, [(0, 0), (0, pad)] + [(0, 0)] * (t.ndim - 2))
    G, R, P, N = SSM_GROUPS, SSM_HEADS_PER_GROUP, SSM_HEAD_DIM, D_STATE
    xdt = padt(xs.astype(f32) * dt[..., None]).reshape(Bsz, nc, lc, G, R, P)
    dA = padt(dt * A).reshape(Bsz, nc, lc, G, R)
    Bc = padt(Bm.astype(f32)).reshape(Bsz, nc, lc, G, N)
    Cc = padt(Cm.astype(f32)).reshape(Bsz, nc, lc, G, N)
    a_cum = jnp.cumsum(dA, axis=2)
    causal = jnp.tril(jnp.ones((lc, lc), dtype=bool))[None, None, :, :, None, None]
    seg = a_cum[:, :, :, None] - a_cum[:, :, None, :]
    decay_ls = jnp.exp(jnp.where(causal, seg, -jnp.inf))
    cb = jnp.einsum('bclgn,bcsgn->bclsg', Cc, Bc)
    y_diag = jnp.einsum('bclsg,bclsgr,bcsgrp->bclgrp', cb, decay_ls, xdt)
    decay_end = jnp.exp(a_cum[:, :, -1:] - a_cum)
    chunk_states = jnp.einsum('bclgn,bclgr,bclgrp->bcgrpn', Bc, decay_end, xdt)
    chunk_decay = jnp.exp(a_cum[:, :, -1])

    def step(h, inp):
        dec, st = inp
        return dec[..., None, None] * h + st, h

    h_last, h_prev = lax.scan(step, h0.astype(f32).reshape(Bsz, G, R, P, N),
                              (jnp.moveaxis(chunk_decay, 1, 0), jnp.moveaxis(chunk_states, 1, 0)))
    h_prev = jnp.moveaxis(h_prev, 0, 1)
    y_off = jnp.einsum('bclgn,bcgrpn,bclgr->bclgrp', Cc, h_prev, jnp.exp(a_cum))
    y = (y_diag + y_off).reshape(Bsz, nc * lc, SSM_HEADS, P)[:, :T]
    return y, h_last.reshape(Bsz, SSM_HEADS, P, N)

def dilated_attention_prompt(q, k, v, window, dil, slopes):
    f32 = jnp.float32
    Bsz, T, Hg, dh = q.shape
    steps = window // dil
    L = T // dil
    nb = -(-L // steps)
    Lp = nb * steps

    def by_residue(t, front):
        t = t.reshape(Bsz, L, dil, Hg, dh)
        return jnp.pad(t, ((0, 0), (front, Lp - L), (0, 0), (0, 0), (0, 0)))

    def key_blocks(t):
        tb = by_residue(t, steps).reshape(Bsz, nb + 1, steps, dil, Hg, dh)
        return jnp.concatenate([tb[:, :-1], tb[:, 1:]], axis=2)

    scale = ATTN_HEAD_DIM ** -0.5
    qb = by_residue(q * scale, 0).reshape(Bsz, nb, steps, dil, Hg, dh)
    kb, vb = key_blocks(k), key_blocks(v)
    i = jnp.arange(steps)[:, None]
    j = jnp.arange(2 * steps)[None, :]
    d_sub = i + steps - j
    key_sub = jnp.arange(nb)[:, None, None] * steps + j[None] - steps
    valid = (d_sub >= 0) & (d_sub <= steps) & (key_sub >= 0)
    dist = (d_sub * dil).astype(f32)
    s = jnp.einsum('bnidhe,bnjdhe->bndhij', qb, kb, preferred_element_type=f32)
    s = s - slopes[:, None, None] * dist
    s = jnp.where(valid[None, :, None, None], s, -jnp.inf)
    lse = jax.nn.logsumexp(s, axis=-1)
    p = jnp.exp(s - lse[..., None])
    o = jnp.einsum('bndhij,bnjdhe->bnidhe', p.astype(vb.dtype), vb, preferred_element_type=f32)
    o = o.reshape(Bsz, Lp, dil, Hg, dh)[:, :L].reshape(Bsz, T, Hg, dh)
    lse = jnp.moveaxis(lse, -1, 2).reshape(Bsz, Lp, dil, Hg)[:, :L].reshape(Bsz, T, Hg)
    kv = jnp.stack([k, v], axis=2)[:, max(T - window, 0):]
    kv = jnp.pad(kv, ((0, 0), (window - kv.shape[1], 0), (0, 0), (0, 0), (0, 0)))
    return o, lse, kv

def dilated_attention_sample(q, k, v, kv_buf, window, dil, slopes):
    f32 = jnp.float32
    Bsz, T, Hg, dh = q.shape
    steps = window // dil
    kv_all = jnp.concatenate([kv_buf.astype(k.dtype), jnp.stack([k, v], axis=2)], axis=1)
    back = jnp.arange(steps + 1) * dil
    idx = window + jnp.arange(T)[:, None] - back[None]
    kv_sel = kv_all[:, idx]
    valid = (PAST_LEN + jnp.arange(T)[:, None] - back[None]) >= 0
    s = jnp.einsum('bthe,btihe->bthi', q * (ATTN_HEAD_DIM ** -0.5), kv_sel[:, :, :, 0], preferred_element_type=f32)
    s = s - slopes[:, None] * back.astype(f32)
    s = jnp.where(valid[None, :, None, :], s, -jnp.inf)
    lse = jax.nn.logsumexp(s, axis=-1)
    p = jnp.exp(s - lse[..., None])
    o = jnp.einsum('bthi,btihe->bthe', p.astype(kv_sel.dtype), kv_sel[:, :, :, 1], preferred_element_type=f32)
    return o, lse, kv_all[:, T:]

def token_mixer(u, conv_buf, h0, kv_bufs, is_prompt, w_in, conv_w, conv_b, dt_bias, a_log, d_skip,
                ssm_norm_g, w_out_ssm, w_out_attn, w_out):
    Bsz, T, _ = u.shape
    proj = u @ w_in
    cuts = [int(c) for c in np.cumsum(PROJ_SIZES)[:-1]]
    z, xbc, dt_raw, q, k, v, gate_a, gate_b = jnp.split(proj, cuts, axis=-1)
    xbc_ext = jnp.concatenate([conv_buf.astype(xbc.dtype), xbc], axis=1)
    new_conv = xbc_ext[:, -(CONV_WIDTH - 1):]
    xbc_c = jax.nn.silu(causal_dwconv(xbc_ext, conv_w, conv_b))
    xs, Bm, Cm = jnp.split(xbc_c, [D_INNER, D_INNER + SSM_GROUPS * D_STATE], axis=-1)
    xs = xs.reshape(Bsz, T, SSM_HEADS, SSM_HEAD_DIM)
    Bm = Bm.reshape(Bsz, T, SSM_GROUPS, D_STATE)
    Cm = Cm.reshape(Bsz, T, SSM_GROUPS, D_STATE)
    dt = jax.nn.softplus(dt_raw.astype(jnp.float32) + dt_bias)
    A = -jnp.exp(a_log.astype(jnp.float32))
    y, h_new = ssd_scan(xs, dt, A, Bm, Cm, h0)
    y = y + d_skip[:, None] * xs
    y = y.reshape(Bsz, T, D_INNER) * jax.nn.silu(z.astype(jnp.float32))
    branch_a = group_rms_norm(y, ssm_norm_g).astype(u.dtype) @ w_out_ssm
    q = q.reshape(Bsz, T, N_ATTN_HEADS, ATTN_HEAD_DIM)
    k = k.reshape(Bsz, T, N_ATTN_HEADS, ATTN_HEAD_DIM)
    v = v.reshape(Bsz, T, N_ATTN_HEADS, ATTN_HEAD_DIM)
    slopes = alibi_slopes()
    outs, lses, new_kv = [], [], []
    for g, (window, dil) in enumerate(DIL_GROUPS):
        hs = slice(g * HEADS_PER_DIL_GROUP, (g + 1) * HEADS_PER_DIL_GROUP)
        if is_prompt:
            o, lse, kvb = dilated_attention_prompt(q[:, :, hs], k[:, :, hs], v[:, :, hs], window, dil, slopes[hs])
        else:
            o, lse, kvb = dilated_attention_sample(q[:, :, hs], k[:, :, hs], v[:, :, hs], kv_bufs[g], window, dil, slopes[hs])
        outs.append(o)
        lses.append(lse)
        new_kv.append(kvb)
    w_groups = jax.nn.softmax(jnp.stack(lses, axis=0), axis=0)
    o = jnp.einsum('gbth,gbthe->bthe', w_groups, jnp.stack(outs, axis=0))
    branch_b = o.reshape(Bsz, T, ATTN_OUT_WIDTH).astype(u.dtype) @ w_out_attn
    merged = jax.nn.sigmoid(gate_a) * branch_a + jax.nn.sigmoid(gate_b) * branch_b
    return merged @ w_out, new_conv, h_new, new_kv

def moe_ffn(x, w_router, b_router, w_gate_up, b_gate_up, w_down, b_down):
    shp = x.shape
    xt = x.reshape(-1, D_MODEL)
    n_tok = xt.shape[0]
    logits = (xt @ w_router).astype(jnp.float32) + b_router
    top_val, top_idx = lax.top_k(logits, TOP_K)
    gates = jax.nn.softmax(top_val, axis=-1)
    n_asg = n_tok * TOP_K
    e_flat = top_idx.reshape(-1)
    tok_flat = jnp.arange(n_asg, dtype=jnp.int32) // TOP_K
    order = jnp.argsort(e_flat)
    e_s, tok_s, g_s = e_flat[order], tok_flat[order], gates.reshape(-1)[order]
    counts = jnp.bincount(e_flat, length=N_EXPERTS)
    start = jnp.cumsum(counts) - counts
    padded = (counts + MOE_BLOCK - 1) // MOE_BLOCK * MOE_BLOCK
    pend = jnp.cumsum(padded)
    pstart = pend - padded
    dest = pstart[e_s] + jnp.arange(n_asg) - start[e_s]
    n_blk = -(-n_asg // MOE_BLOCK) + N_EXPERTS
    n_slot = n_blk * MOE_BLOCK
    buf_tok = jnp.full((n_slot,), n_tok, dtype=jnp.int32).at[dest].set(tok_s)
    buf_g = jnp.zeros((n_slot,), jnp.float32).at[dest].set(g_s)
    blk_exp = jnp.minimum(jnp.searchsorted(pend, jnp.arange(n_blk) * MOE_BLOCK, side='right'), N_EXPERTS - 1)
    xpad = jnp.concatenate([xt, jnp.zeros((1, D_MODEL), xt.dtype)], axis=0)

    def run_block(args):
        tok_b, g_b, e = args
        h = xpad[tok_b] @ w_gate_up[e] + b_gate_up[e]
        gate, up = h[:, :D_FF], h[:, D_FF:]
        gate = jnp.minimum(gate, SWIGLU_LIMIT)
        up = jnp.clip(up, -SWIGLU_LIMIT, SWIGLU_LIMIT)
        hmid = (up + 1.0) * (gate * jax.nn.sigmoid(SWIGLU_ALPHA * gate))
        out = hmid @ w_down[e] + b_down[e]
        return out * g_b[:, None].astype(out.dtype)

    outs = lax.map(run_block, (buf_tok.reshape(n_blk, MOE_BLOCK), buf_g.reshape(n_blk, MOE_BLOCK), blk_exp))
    y = jax.ops.segment_sum(outs.reshape(n_slot, D_MODEL), buf_tok, num_segments=n_tok + 1)[:n_tok]
    return y.reshape(shp).astype(x.dtype)

def decoder_layer(x, conv_buf, h0, kv_bufs, is_prompt, w_in, conv_w, conv_b, dt_bias, a_log, d_skip, ssm_norm_g,
                  w_out_ssm, w_out_attn, w_out, ln1_g, ln1_b, w_router, b_router, w_gate_up, b_gate_up, w_down,
                  b_down, ln2_g, ln2_b):
    mix, new_conv, h_new, new_kv = token_mixer(x, conv_buf, h0, kv_bufs, is_prompt, w_in, conv_w, conv_b, dt_bias,
                                               a_log, d_skip, ssm_norm_g, w_out_ssm, w_out_attn, w_out)
    x1 = layer_norm(ALPHA * x + mix.astype(x.dtype), ln1_g, ln1_b)
    x2 = layer_norm(ALPHA * x1 + moe_ffn(x1, w_router, b_router, w_gate_up, b_gate_up, w_down, b_down), ln2_g, ln2_b)
    return x2, h_new, new_conv, new_kv

def setup_inputs(seed: int = 0) -> dict:
    key = jax.random.key(seed)
    ks = jax.random.split(key, 32)
    f32 = jnp.float32
    nrm = lambda k, shape, s: jax.random.normal(k, shape, f32) * s
    L = DEPTH
    Hg, dh = HEADS_PER_DIL_GROUP, ATTN_HEAD_DIM
    v_lo = D_INNER + CONV_DIM + SSM_HEADS + 2 * ATTN_WIDTH
    col_scale = jnp.ones((D_IN_PROJ,), f32).at[v_lo:v_lo + ATTN_WIDTH].set(BETA)
    dt0 = jnp.exp(jax.random.uniform(ks[10], (L, SSM_HEADS), f32, np.log(1e-3), np.log(1e-1)))
    return {
        "x_prompt": nrm(ks[0], (BATCH, SEQ, D_MODEL), 1.0),
        "x_sample": nrm(ks[1], (DEC_BATCH, DEC_SEQ, D_MODEL), 1.0),
        "state_ssm": nrm(ks[2], (L, DEC_BATCH, SSM_HEADS, SSM_HEAD_DIM, D_STATE), 0.5),
        "state_conv": nrm(ks[3], (L, DEC_BATCH, CONV_WIDTH - 1, CONV_DIM), 1.0),
        "cache_kv_w128": nrm(ks[4], (L, DEC_BATCH, DIL_GROUPS[0][0], 2, Hg, dh), 1.0),
        "cache_kv_w512": nrm(ks[5], (L, DEC_BATCH, DIL_GROUPS[1][0], 2, Hg, dh), 1.0),
        "cache_kv_w2048": nrm(ks[6], (L, DEC_BATCH, DIL_GROUPS[2][0], 2, Hg, dh), 1.0),
        "w_in": nrm(ks[7], (L, D_MODEL, D_IN_PROJ), D_MODEL ** -0.5) * col_scale,
        "conv_w": nrm(ks[8], (L, CONV_WIDTH, CONV_DIM), CONV_WIDTH ** -0.5),
        "conv_b": nrm(ks[9], (L, CONV_DIM), 0.02),
        "dt_bias": dt0 + jnp.log(-jnp.expm1(-dt0)),
        "a_log": jnp.log(jax.random.uniform(ks[11], (L, SSM_HEADS), f32, 1.0, 16.0)),
        "d_skip": 1.0 + nrm(ks[12], (L, SSM_HEADS), 0.02),
        "ssm_norm_g": 1.0 + nrm(ks[13], (L, D_INNER), 0.02),
        "w_out_ssm": nrm(ks[14], (L, D_INNER, D_MODEL), D_INNER ** -0.5),
        "w_out_attn": nrm(ks[15], (L, ATTN_OUT_WIDTH, D_MODEL), ATTN_OUT_WIDTH ** -0.5),
        "w_out": nrm(ks[16], (L, D_MODEL, D_MODEL), BETA * D_MODEL ** -0.5),
        "ln1_g": 1.0 + nrm(ks[17], (L, D_MODEL), 0.02),
        "ln1_b": nrm(ks[18], (L, D_MODEL), 0.02),
        "w_router": nrm(ks[19], (L, D_MODEL, N_EXPERTS), D_MODEL ** -0.5),
        "b_router": nrm(ks[20], (L, N_EXPERTS), 0.01),
        "w_gate_up": nrm(ks[21], (L, N_EXPERTS, D_MODEL, 2 * D_FF), D_MODEL ** -0.5),
        "b_gate_up": nrm(ks[22], (L, N_EXPERTS, 2 * D_FF), 0.02),
        "w_down": nrm(ks[23], (L, N_EXPERTS, D_FF, D_MODEL), BETA * D_FF ** -0.5),
        "b_down": nrm(ks[24], (L, N_EXPERTS, D_MODEL), 0.02),
        "ln2_g": 1.0 + nrm(ks[25], (L, D_MODEL), 0.02),
        "ln2_b": nrm(ks[26], (L, D_MODEL), 0.02),
    }

def reference(x_prompt, x_sample, state_ssm, state_conv, cache_kv_w128, cache_kv_w512, cache_kv_w2048, w_in, conv_w,
              conv_b, dt_bias, a_log, d_skip, ssm_norm_g, w_out_ssm, w_out_attn, w_out, ln1_g, ln1_b, w_router,
              b_router, w_gate_up, b_gate_up, w_down, b_down, ln2_g, ln2_b):
    y_p, y_s = x_prompt, x_sample
    bp = x_prompt.shape[0]
    p_states, s_states = [], []
    for l in range(DEPTH):
        lw = (w_in[l], conv_w[l], conv_b[l], dt_bias[l], a_log[l], d_skip[l], ssm_norm_g[l], w_out_ssm[l],
              w_out_attn[l], w_out[l], ln1_g[l], ln1_b[l], w_router[l], b_router[l], w_gate_up[l], b_gate_up[l],
              w_down[l], b_down[l], ln2_g[l], ln2_b[l])
        conv0 = jnp.zeros((bp, CONV_WIDTH - 1, CONV_DIM), x_prompt.dtype)
        h0 = jnp.zeros((bp, SSM_HEADS, SSM_HEAD_DIM, D_STATE), jnp.float32)
        y_p, hp, cp, kvp = decoder_layer(y_p, conv0, h0, None, True, *lw)
        y_s, hs, cs, kvs = decoder_layer(y_s, state_conv[l], state_ssm[l],
                                         (cache_kv_w128[l], cache_kv_w512[l], cache_kv_w2048[l]), False, *lw)
        p_states.append((hp, cp, kvp[0], kvp[1], kvp[2]))
        s_states.append((hs, cs, kvs[0], kvs[1], kvs[2]))
    prompt_ssm = jnp.stack([st[0] for st in p_states])
    prompt_conv = jnp.stack([st[1] for st in p_states])
    prompt_kv_w128 = jnp.stack([st[2] for st in p_states])
    prompt_kv_w512 = jnp.stack([st[3] for st in p_states])
    prompt_kv_w2048 = jnp.stack([st[4] for st in p_states])
    sample_ssm = jnp.stack([st[0] for st in s_states])
    sample_conv = jnp.stack([st[1] for st in s_states])
    sample_kv_w128 = jnp.stack([st[2] for st in s_states])
    sample_kv_w512 = jnp.stack([st[3] for st in s_states])
    sample_kv_w2048 = jnp.stack([st[4] for st in s_states])
    return (y_p, y_s, prompt_ssm, prompt_conv, prompt_kv_w128, prompt_kv_w512, prompt_kv_w2048,
            sample_ssm, sample_conv, sample_kv_w128, sample_kv_w512, sample_kv_w2048)


_drawn_inputs = setup_inputs


def setup_inputs(seed=0):
    import zlib

    import numpy as np

    out = dict(_drawn_inputs(seed))
    spreads = {}
    factors = {'d_skip': 5.709,
     'ssm_norm_g': 5.156,
     'b_gate_up': 8.0,
     'b_down': 6.414,
     'ln2_g': 2.801,
     'ln2_b': 2.803}
    for name, (base, spread) in spreads.items():
        noise = np.random.default_rng([zlib.crc32(name.encode()), seed]).standard_normal(out[name].shape)
        drawn = base * np.exp(spread * noise) if base else spread * noise
        out[name] = __import__('jax').numpy.asarray(drawn.astype(out[name].dtype))
    for name, factor in factors.items():
        out[name] = (out[name] * factor).astype(out[name].dtype)
    return out
```

```python
from contextlib import ExitStack

import numpy as np

import concourse.bass as bass
from concourse import mybir

F32 = mybir.dt.float32
F32R = mybir.dt.float32r
I32 = mybir.dt.int32
U32 = mybir.dt.uint32
ALU = mybir.AluOpType
ACT = mybir.ActivationFunctionType
X = mybir.AxisListType.X

P = 128
D = 1024
KT = D // P
TP, TS = 256, 8
T = TP + TS
INNER, HEADS, HP, NST, GROUPS = 2048, 32, 64, 128, 4
HPG = HEADS // GROUPS
CONV_DIM, CW = 3072, 4
CHUNK = 128
ZT, XT, QT, GT = 16, 24, 18, 16
Z0, X0, B0, C0 = 0, ZT, ZT + 16, ZT + 20
Q0, K0, V0, G0 = 40, 46, 52, 58
NT = 74
DT_COL = INNER + CONV_DIM
NH, DH, HG = 12, 64, 4
DIL = ((128, 1), (512, 4), (2048, 16))
PAST = 1024
SCALE = DH ** -0.5
SLOPES = [float(np.float32(2.0 ** (-8.0 * i / NH))) for i in range(1, NH + 1)]
NEG = -1e30
EPS = 1e-5
ALPHA = 2.0 ** 0.25
NE, TOPK, FF = 32, 4, 1024
LIMIT, SW_ALPHA = 7.0, 1.702
BLK = 64
MAX_OV = 16
MAX_BLK = NE + MAX_OV
CH = 2048
RING = 6
HL, HL_PROJ = 4, 3
N_PROJ = 37
N_SSM, N_ATT, N_OUT = 8, 1, 4
NATIVE0 = N_PROJ
MOE0 = N_PROJ + N_SSM + N_ATT + N_OUT
HSN = 3
GU_CH, DN_CH = 8, 4
STEP0 = MOE0 - 4
CREDIT = 12


def bc(ap, shape):
    return ap.broadcast_to(shape)


def build(nc, x_prompt, x_sample, state_ssm, state_conv, cache_kv_w128, cache_kv_w512, cache_kv_w2048, w_in,
          conv_w, conv_b, dt_bias, a_log, d_skip, ssm_norm_g, w_out_ssm, w_out_attn, w_out, ln1_g, ln1_b,
          w_router, b_router, w_gate_up, b_gate_up, w_down, b_down, ln2_g, ln2_b,
          y_prompt, y_sample, prompt_ssm, prompt_conv, prompt_kv0, prompt_kv1, prompt_kv2,
          sample_ssm, sample_conv, sample_kv0, sample_kv1, sample_kv2):
    caches = (cache_kv_w128, cache_kv_w512, cache_kv_w2048)
    prompt_kv = (prompt_kv0, prompt_kv1, prompt_kv2)
    sample_kv = (sample_kv0, sample_kv1, sample_kv2)
    q_scratch = nc.dram_tensor("q_scratch", (TS, NH * DH), F32, kind="Internal").ap()
    rows_scratch = nc.dram_tensor("rows_scratch", (MAX_BLK * BLK, D), F32, kind="Internal").ap()

    keep = ExitStack()
    sems = {}

    def S(name):
        if name not in sems:
            sems[name] = keep.enter_context(nc.semaphore(name))
        return sems[name]

    class Chain:

        def __init__(self, eng, name):
            self.eng, self.sem, self.n = eng, S(name), 0

        def then(self, ins):
            self.n = self.n + 1
            ins.then_inc(self.sem, 1)
            self.eng.wait_ge(self.sem, self.n)

    with keep:
        def sb(stack, name, shape, dt=F32):
            return stack.enter_context(nc.sbuf_tensor(name, shape, dt))

        psum = keep.enter_context(nc.psum_tensor("psum", [P, 8, 512], F32))
        bank = [psum[:, i, :] for i in range(8)]

        STAGES = {
            "act_stage": ("aln_done", "aw_done", "sexp_done", "sln_done", "sw_done", "so_copied", "x1h_done",
                          "gexp_done", "gmT_ready"),
            "dve_stage": ("dt_abs", "acum_ready", "ys_done", "norm_done", "adiff_ready", "coef_ready",
                          "sarg_ready", "ssum_ready", "sdiff_ready", "sp_ready", "selfo_ready", "x1_ready",
                          "x1l_done", "mask_ready", "gdiff_ready", "gm_ready", "table_ready"),
            "pe_stage": ("params_psum", "dt_raw", "dt_psum", "qkvs_psum", "sturn_psum", "pj_psum", "so_psum",
                          "logits_psum", "rank_psum", "gmT_psum"),
        }

        def stage(name):
            return S(next(s for s, names in STAGES.items() if name in names))

        def reached(name):
            s, names = next((s, names) for s, names in STAGES.items() if name in names)
            return S(s), names.index(name) + 1

        ident = sb(keep, "ident", [P, P])
        ones = sb(keep, "ones", [P, P])
        fold = sb(keep, "fold", [P, BLK])
        later = sb(keep, "later", [P, P])
        iota64 = sb(keep, "iota64", [P, BLK])
        zero = sb(keep, "zero", [P, 512])
        step64 = sb(keep, "step64", [P, 1])
        credit = sb(keep, "credit", [1, 4])
        with ExitStack() as raw:
            wraw = sb(raw, "wraw", [P, RING, CH])
        wlow = sb(keep, "wlow", [P, RING, CH], F32R)
        wh = sb(keep, "wh", [P, HL, CH], F32R)
        bgu = sb(keep, "bgu", [P, 2 * KT, NE])

        mixer = ExitStack()
        proj = sb(mixer, "proj", [P, NT, T])

        def over(tile, partitions, words):
            n = -(-words // T)
            return proj[0:partitions, tile:tile + n, :].rearrange("p a b -> p (a b)")[:, 0:words]

        x_tok = over(G0, P, 3 * D).rearrange("p (t d) -> p t d", t=3)
        rows = over(Q0, 29, CONV_DIM)
        gn_rows = over(V0, ZT, P)
        bgu_rows = over(X0, NE, 2 * FF)
        xT = proj[:, X0 + 12:X0 + 12 + KT, :]
        dts = proj[0:HEADS, Q0:Q0 + 8, :]
        kvtok = over(X0, P, 2 * 12 * P).rearrange("p (t f c) -> p t f c", t=2, f=12)
        vsel = over(X0, P, 3 * TS * 256).rearrange("p (g b c) -> p g b c", g=3, b=TS)
        def pair(ap):
            return ap.rearrange("p (i b c) -> p i b c", i=2, b=TS)

        kq_even = pair(over(Q0, P, 2 * TS * 256))
        sprod = over(X0, P, 2 * ZT * P).rearrange("p (i f n) -> p i f n", i=2, f=ZT)
        acum = sb(mixer, "acum", [HEADS, 2, P])
        hcol = sb(mixer, "hcol", [HEADS, 8])
        dtok = sb(mixer, "dtok", [P, 6, HEADS])
        feat = sb(mixer, "feat", [P, ZT, 17])
        gn = sb(mixer, "gn", [P, ZT])
        dec1 = sb(mixer, "dec1", [P, HEADS])
        with ExitStack() as early:
            xh = sb(early, "xh", [P, KT, T], F32R)
            xl = sb(early, "xl", [P, KT, T], F32R)
            wdt = sb(early, "wdt", [P, KT, HEADS])
            cs = sb(early, "cs", [P, XT, 32])
            ctmp = sb(early, "ctmp", [P, 2, T])
            csig = sb(early, "csig", [P, 2, T])
            tail = sb(early, "tail", [11, XT, P])
        with ExitStack() as ssd:
            lmat = sb(ssd, "lmat", [P, 2, HPG, P])
            xdt = sb(ssd, "xdt", [P, 2, 512])
            xw = sb(ssd, "xw", [P, 2, 512])
            btok = sb(ssd, "btok", [P, 2, P])
            cbm = sb(ssd, "cbm", [P, 2, P])
            ctile = sb(ssd, "ctile", [P, 2, HPG, P])
            s0 = sb(ssd, "s0", [P, INNER])
            hT = sb(ssd, "hT", [P, 512])
            hout = sb(ssd, "hout", [P, 4, P])
            yt = sb(ssd, "yt", [P, 512])
        with ExitStack() as ssm:
            hs = sb(ssm, "hs", [P, HSN, ZT, P])
            xdts = sb(ssm, "xdts", [P, ZT, TS])
            xskip = sb(ssm, "xskip", [P, ZT, TS])
            ysum = sb(ssm, "ysum", [P, ZT, TS])
        with ExitStack() as norm:
            ysq = sb(norm, "ysq", [P, ZT, T])
            rstd = sb(norm, "rstd", [P, GROUPS, T])
        abuf = ExitStack()
        oT = sb(abuf, "oT", [P, 2, T])
        qkvs = sb(abuf, "qkvs", [TS, QT, P])
        with ExitStack() as att:
            pa = sb(att, "pa", [P, NH, 3 * P])
            pT = sb(att, "pT", [P, 2, 3 * P])
            rel = sb(att, "rel", [P, 3 * P])
            masks = sb(att, "masks", [P, 3, 3 * P])
            bias = sb(att, "bias", [P, 2, 3 * P])
            reli = bias[:, 0, :].bitcast(I32)
            relb = bias[:, 1, :].bitcast(I32)
            ast = sb(att, "ast", [P, 8, 2, NH])
        with ExitStack() as satt:
            kq_odd = sb(satt, "kq_odd", [P, 2, TS, 256])
            ss = sb(satt, "ss", [TS, NH, P + 1])
            sback = sb(satt, "sback", [TS, P])
            sst = sb(satt, "sst", [TS, 8, NH])
            stok = sb(satt, "stok", [P, NH, TS])
            pj = sb(satt, "pj", [P, NH, TS])
            selfo = sb(satt, "selfo", [TS, NH * DH])
        kq = (kq_even, kq_odd, kq_even)
        abuf.close()
        mixer.close()

        moe = ExitStack()
        x1 = sb(moe, "x1", [P, 3, D])
        x1h = sb(moe, "x1h", [P, 3, D], F32R)
        x1l = sb(moe, "x1l", [P, 3, D], F32R)
        with ExitStack() as merge:
            merged = sb(merge, "merged", [P, KT, T])
            bpart = sb(merge, "bpart", [P, KT, T])
        hcopy = sb(moe, "hcopy", [P, 2 * FF])
        xst = sb(moe, "xst", [P, KT, P], F32R)
        hst = sb(moe, "hst", [P, KT, P], F32R)
        gg = sb(moe, "gg", [P, KT, BLK])
        uu = sb(moe, "uu", [P, KT, BLK])
        sg = sb(moe, "sg", [P, KT, BLK])
        low = sb(moe, "low", [BLK, D])
        orow = sb(moe, "orow", [BLK, D])
        oneh = sb(moe, "oneh", [P, 3, BLK], F32R)
        bcur = sb(moe, "bcur", [P, 2 * KT])
        xres = sb(moe, "xres", [P, 3, D])
        lnp = sb(moe, "lnp", [P, 2, D])
        bdn = sb(moe, "bdn", [NE, D])
        wr = sb(moe, "wr", [P, KT, NE])
        br = sb(moe, "br", [P, NE])
        lg = sb(moe, "lg", [P, 3, NE])
        mx = sb(moe, "mx", [P, 3, 8])
        ix = sb(moe, "ix", [P, 3, 8], U32)
        ixf = sb(moe, "ixf", [P, 3, 8])
        gate = sb(moe, "gate", [P, 3, TOPK])
        gsum = sb(moe, "gsum", [P, 3])
        pick = sb(moe, "pick", [P, 3, TOPK, NE])
        pick2 = sb(moe, "pick2", [P, 3, TOPK, NE])
        mask = sb(moe, "mask", [P, 3, NE])
        gm = sb(moe, "gm", [P, 3, NE])
        gmT = sb(moe, "gmT", [NE, T])
        strict = sb(moe, "strict", [P, P])
        ecol = sb(moe, "ecol", [P, NE])
        rank = sb(moe, "rank", [P, 4, NE])
        cnt = sb(moe, "cnt", [P, 6, NE])
        slot = sb(moe, "slot", [P, 3, NE])
        slotj = sb(moe, "slotj", [P, 3, TOPK])
        slotu = sb(moe, "slotu", [P, 3, TOPK], U32)
        sl = sb(moe, "sl", [P, 3])
        blkbase = sb(moe, "blkbase", [P, 1])
        ovc = sb(moe, "ovc", [1, MAX_OV, NE])
        tabf = sb(moe, "tabf", [1, MAX_BLK + 4])
        tab = sb(moe, "tab", [1, MAX_BLK + 4], I32)
        lnst = sb(moe, "lnst", [P, 3, 16])
        x1T = xres[:, :, :].rearrange("p a b -> p (a b)")[:, 0:KT * T].rearrange("p (k t) -> p k t", k=KT)
        moe.close()
        w_in_v = w_in[0].rearrange("(k p) n -> p k n", p=P)
        wgu = w_gate_up[0]
        wdn = w_down[0]

        def raw_ready(eng, n, rep=0, per=0):
            eng.wait_ge(S(f"raw_landed{n % RING}"), 16 * (n // RING + 1) + 16 * (per // RING) * rep)

        def split_no(n):
            return n if n < NATIVE0 else n - (MOE0 - NATIVE0)

        def used(n, b=0):
            return CREDIT + n - MOE0 + 1 + 12 * b

        def high_slot(n):
            return n % HL_PROJ if n < NATIVE0 else (n - MOE0) % HL

        def act_high(act, n, rep=0, per=0):
            raw_ready(act, n, rep, per)
            if HL_PROJ <= n < NATIVE0:
                act.wait_ge(S("tile_done"), 2 * (n - HL_PROJ + 1) + 2 * per * rep)
            elif n >= MOE0 + HL or per == 12:
                act.wait_ge(S("split_used"), used(n - HL, rep))
            nc.scalar.activation(wh[:, high_slot(n), :], wraw[:, n % RING, :], ACT.Copy).then_inc(S("high_done"), 1)

        def dve_low(dve, n, rep=0, per=0):
            dve.wait_ge(S("high_done"), split_no(n) + 1 + per * rep)
            nc.vector.tensor_tensor(wlow[:, n % RING, :], wraw[:, n % RING, :], wh[:, high_slot(n), :].bitcast(F32),
                                    ALU.subtract).then_inc(S("low_done"), 1)

        def pe_split(pe, n, rep=0, per=0):
            pe.wait_ge(S("low_done"), split_no(n) + 1 + per * rep)
            return wh[:, high_slot(n), :], wlow[:, n % RING, :]

        def gate_up_used(b):
            return used(MOE0 + GU_CH - 1) if isinstance(b, int) and b == 0 else used(STEP0 + GU_CH - 1, b)

        RUN1 = (ZT + XT) // 2
        L1, L2 = RUN1 // RING, (N_PROJ - RUN1) // RING

        block = keep.enter_context(nc.Block())

        @block.sync
        def _(sp):
            def native_free(i):
                if i < N_SSM - 1:
                    sp.wait_ge(S("native_used"), i + 1)
                elif i == N_SSM - 1:
                    sp.wait_ge(S("branch_a"), KT)
                elif i == N_SSM:
                    sp.wait_ge(S("branch_b"), KT)
                elif i < N_SSM + N_ATT + N_OUT - 1:
                    sp.wait_ge(S("native_used"), i - 1)
                else:
                    sp.wait_ge(S("mix_psum"), 3)

            def load(n, dst, src):
                sp.dma_start(dst, src).then_inc(S(f"raw_landed{n % RING}"), 16)

            def w_in_chunk(c, col):
                return wraw[:, c % RING, :].rearrange("p (k n) -> p k n", k=KT), w_in_v[:, :, bass.ds(col, 256)]

            for j in range(RING):
                load(j, *w_in_chunk(j, 256 * j))
            with sp.Fori(1, L1) as i:
                for j in range(RING):
                    sp.wait_ge(S("tile_done"), 2 * (j - RING + 1) + 2 * RING * i)
                    load(j, *w_in_chunk(j, 256 * j + 256 * RING * i))
            for c in range(L1 * RING, RUN1):
                sp.wait_ge(S("tile_done"), 2 * (c - RING + 1))
                load(c, *w_in_chunk(c, 256 * c))
            with sp.Fori(0, L2) as i:
                for j in range(RING):
                    c = RUN1 + j
                    sp.wait_ge(S("tile_done"), 2 * (c - RING + 1) + 2 * RING * i)
                    load(c, *w_in_chunk(c, DT_COL + HEADS + 256 * j + 256 * RING * i))
            for c in range(RUN1 + L2 * RING, N_PROJ):
                sp.wait_ge(S("tile_done"), 2 * (c - RING + 1))
                load(c, *w_in_chunk(c, DT_COL + HEADS + 256 * (c - RUN1)))
            native = [(w_out_ssm, 256 * j) for j in range(N_SSM)] + [(w_out_attn, 0)]
            native += [(w_out, 256 * j) for j in range(N_OUT)]
            for j, (w, r) in enumerate(native):
                n = NATIVE0 + j
                if n - RING < NATIVE0:
                    sp.wait_ge(S("tile_done"), 2 * (n - RING + 1))
                else:
                    native_free(n - RING - NATIVE0)
                load(n, wraw[:, n % RING, :].rearrange("p (a n) -> p a n", a=2),
                     w[0, r:r + 256, :].rearrange("(a p) n -> p a n", p=P))

            def gate_up(n, e, k):
                return wraw[:, n % RING, :], wgu[bass.ds(e, 1), k * P:(k + 1) * P, :].rearrange("a p n -> p (a n)")

            def down(n, e, j):
                return (wraw[:, n % RING, :].rearrange("p (a n) -> p a n", a=2),
                        wdn[bass.ds(e, 1), j * 256:(j + 1) * 256, :].rearrange("e (a p) n -> p (e a) n", p=P))

            for k in range(GU_CH):
                n = MOE0 + k
                if n - RING < MOE0:
                    native_free(n - RING - NATIVE0)
                else:
                    sp.wait_ge(S("split_used"), used(n - RING))
                load(n, *gate_up(n, 0, k))

            def block_chunks(b, e, e_before):
                for c in range(12):
                    n = STEP0 + c
                    sp.wait_ge(S("split_used"), used(n - RING, b))
                    if c < GU_CH:
                        load(n, *gate_up(n, e, c))
                    else:
                        load(n, *down(n, e_before, c - GU_CH))

            with sp.Fori(1, NE) as b:
                block_chunks(b, b, b - 1)
            sp.wait_ge(*reached("table_ready"))
            nblk = sp.value_load(tab[0:1, MAX_BLK + 3:MAX_BLK + 4], min_val=NE, max_val=MAX_BLK)
            more = sp.value_load(tab[0:1, MAX_BLK + 2:MAX_BLK + 3], min_val=0, max_val=1)
            with sp.If(more):
                with sp.Fori(NE, nblk) as b:
                    e = sp.value_load(tab[0:1, bass.ds(b, 1)], min_val=0, max_val=NE - 1)
                    before = sp.value_load(tab[0:1, bass.ds(b - 1, 1)], min_val=0, max_val=NE - 1)
                    block_chunks(b, e, before)
            last = sp.value_load(tab[0:1, bass.ds(nblk - 1, 1)], min_val=0, max_val=NE - 1)
            for j in range(DN_CH):
                n = STEP0 + j
                sp.wait_ge(S("split_used"), used(n - RING, nblk))
                load(n, *down(n, last, j))

        @block.gpsimd
        def _(pool):
            own = Chain(pool, "pool_chain")
            g = nc.gpsimd
            g.memset(ones[:, :], 1.0).then_inc(S("ones_ready"), 1)
            g.memset(step64[:, :], float(BLK)).then_inc(S("split_used"), CREDIT)
            g.memset(credit[:, 0:1], 0.0).then_inc(S("bank_free"), 4)
            g.memset(credit[:, 1:2], 0.0).then_inc(S("conv_done"), 1)
            g.memset(credit[:, 2:3], 0.0).then_inc(S("low_read"), 1)
            g.memset(zero[:, :], 0.0).then_inc(S("zero_ready"), 1)
            g.memset(ident[:, :], 0.0).then_inc(S("pool_z"), 1)
            g.memset(fold[:, :], 0.0).then_inc(S("pool_z"), 1)
            pool.wait_ge(S("pool_z"), 2)
            g.affine_select(out=ident[:, :], in_=ident[:, :], compare_op=ALU.not_equal, fill=1.0, base=0,
                            pattern=[[-1, P]], channel_multiplier=1).then_inc(S("ident_ready"), 1)
            g.dma_start(rows[0:CW, :], conv_w[0]).then_inc(S("rows_in"), 16)
            g.dma_start(rows[CW:CW + 1, :], conv_b).then_inc(S("rows_in"), 16)
            g.dma_start(rows[5:29, :], state_conv[0].rearrange("b j c -> (b j) c")).then_inc(S("rows_in"), 16)
            g.dma_start(bgu_rows, b_gate_up[0]).then_inc(S("rows_in"), 16)
            g.dma_start(gn_rows, ssm_norm_g[0].rearrange("(a b) -> a b", b=P)).then_inc(S("rows_in"), 16)
            with nc.allow_non_contiguous_dma(reason="32 words"):
                g.dma_start(hcol[:, 0:1], dt_bias.rearrange("a h -> h a")).then_inc(S("cols_in"), 16)
                g.dma_start(hcol[:, 1:2], a_log.rearrange("a h -> h a")).then_inc(S("cols_in"), 16)
                g.dma_start(hcol[:, 3:4], d_skip.rearrange("a h -> h a")).then_inc(S("cols_in"), 16)
            own.then(g.memset(later[:, :], 1.0))
            own.then(g.affine_select(out=fold[:, :], in_=fold[:, :], compare_op=ALU.not_equal, fill=1.0, base=0,
                                     pattern=[[-1, BLK]], channel_multiplier=1))
            g.affine_select(out=fold[:, :], in_=fold[:, :], compare_op=ALU.not_equal, fill=1.0, base=-BLK,
                            pattern=[[-1, BLK]], channel_multiplier=1).then_inc(S("consts_ready"), 1)
            g.affine_select(out=later[:, :], in_=later[:, :], compare_op=ALU.is_ge, fill=0.0, base=0,
                            pattern=[[1, P]], channel_multiplier=-1).then_inc(S("consts_ready"), 1)
            g.iota(iota64[:, :], [[1, BLK]], base=0, channel_multiplier=0,
                   allow_small_or_imprecise_dtypes=True).then_inc(S("consts_ready"), 1)

            def move_cache(b):
                for gi, (w, _) in enumerate(DIL):
                    row = 2 * HG * DH
                    words = (w - 1) * row // 16
                    run = words // max(1, -(-words // 15000))
                    while words % run:
                        run -= 1
                    src = caches[gi][0, b].rearrange("w t h e -> (w t h e)")[row:w * row]
                    dst = sample_kv[gi][0, b].rearrange("w t h e -> (w t h e)")[0:(w - 1) * row]
                    g.dma_start(dst.rearrange("(p r c) -> p r c", p=16, c=run),
                                src.rearrange("(p r c) -> p r c", p=16, c=run)).then_inc(S("copies_out"), 16)

            for b in range(3):
                pool.wait_ge(S("tile_done"), 4 + 12 * b)
                move_cache(b)

            with pool.Fori(0, 12) as i:
                pool.wait_ge(S("csig_done"), i + 1)
                g.tensor_tensor(proj[:, bass.ds(X0 + 2 * i, 2), :], ctmp[:, :, :], csig[:, :, :],
                                ALU.mult).then_inc(S("conv_done"), 1)

            pool.wait_ge(S("zero_ready"), 1)
            g.dma_start(rows_scratch[NE * BLK:, :].rearrange("(p a) (c n) -> p (a c) n", p=P, n=512),
                        bc(zero[:, :].unsqueeze(1), [P, MAX_OV * BLK // P * 2, 512])).then_inc(S("rows_stored"), 16)
            for gi, (w, _) in enumerate(DIL):
                if w > TP:
                    dst = prompt_kv[gi][0, 0, 0:w - TP].rearrange("(p a) t h e -> p a (t h e)", p=P)
                    g.dma_start(dst, bc(zero[:, :].unsqueeze(1), [P, (w - TP) // P, 512])).then_inc(
                        S("copies_out"), 16)
            move_cache(3)

            for gi in range(GROUPS):
                pool.wait_ge(S("cexp_done"), gi + 1)
                ct = proj[:, C0 + gi, P:2 * P].unsqueeze(1)
                g.tensor_tensor(ctile[:, gi % 2, :, :], ctile[:, gi % 2, :, :], bc(ct, [P, HPG, P]),
                                ALU.mult).then_inc(S("ctile_ready"), 1)
                if gi < 1:
                    move_cache(4)

            for b in range(TS):
                pool.wait_ge(S(f"hs_in{b % HSN}"), 16 * (b // HSN + 1))
                h = hs[:, b % HSN, :, :]
                own.then(g.tensor_tensor(h, h, bc(feat[:, :, 8 + b:9 + b], [P, ZT, P]), ALU.mult))
                pool.wait_ge(S("bx_ready"), b + 1)
                g.tensor_tensor(h, h, sprod[:, b % 2, :, :], ALU.add).then_inc(S("hnew_ready"), 1)

            pool.wait_ge(*reached("norm_done"))
            for blk, base in enumerate((0, P, 0)):
                g.iota(reli[:, blk * P:(blk + 1) * P], [[-1, P]], base=base,
                       channel_multiplier=1).then_inc(S("rel_ready"), 1)

            move_cache(5)
            move_cache(6)
            pool.wait_ge(*reached("coef_ready"))
            for hg in range(HG):
                for gi in range(3):
                    h = gi * HG + hg
                    g.tensor_scalar(pa[:, h, 0:P], pa[:, h, 0:P], ast[:, 7, 0, h:h + 1], None, ALU.mult)
                    g.tensor_scalar(pa[:, h, P:3 * P], pa[:, h, P:3 * P], ast[:, 7, 1, h:h + 1], None,
                                    ALU.mult).then_inc(S("pa_ready"), 1)
            pool.wait_ge(S("oT_ready"), 1)
            g.iota(sback[:, :], [[-1, P]], base=P, channel_multiplier=0,
                   allow_small_or_imprecise_dtypes=True).then_inc(S("rel_ready"), 1)
            pool.wait_ge(S("vsel_in"), 48)
            move_cache(7)
            pool.wait_ge(*reached("x1_ready"))
            g.memset(blkbase[:, :], 0.0).then_inc(S("pool_z"), 1)
            own.then(g.tensor_tensor(strict[:, :], later[:, :], ident[:, :], ALU.subtract))
            g.iota(ecol[:, :], [[1, NE]], base=0, channel_multiplier=0,
                   allow_small_or_imprecise_dtypes=True).then_inc(S("ecol_ready"), 1)
            for n in range(MAX_OV):
                last = g.memset(ovc[0:1, n, :], float(n))
            last.then_inc(S("ecol_ready"), 1)
            g.iota(tabf[0:1, 0:MAX_BLK + 4], [[1, MAX_BLK + 4]], base=0, channel_multiplier=0,
                   allow_small_or_imprecise_dtypes=True).then_inc(S("ecol_ready"), 1)
            pool.wait_ge(S("pool_z"), 3)

            pool.wait_ge(*reached("table_ready"))
            nblk = pool.value_load(tab[0:1, MAX_BLK + 3:MAX_BLK + 4], min_val=NE, max_val=MAX_BLK)

            PER = 3

            def expert_of(b):
                return pool.value_load(tab[0:1, bass.ds(b, 1)], min_val=0, max_val=NE - 1)

            def row_in_block(b, e, at):
                g.tensor_tensor(sl[:, :], slot[:, :, bass.ds(e, 1)].rearrange("p t e -> p (t e)"),
                                bc(blkbase[:, 0:1], [P, 3]), ALU.subtract).then_inc(S("sl_ready"), 1)
                pool.wait_ge(S("sl_ready"), b + 1)
                g.tensor_tensor(blkbase[:, :], blkbase[:, :], step64[:, :], ALU.add).then_inc(S("pool_steps"), 1)
                pool.wait_ge(S("pool_steps"), at + 1)

            def glu(b_before, at):
                pool.wait_ge(S("up_in"), b_before + 1)
                g.tensor_tensor(uu[:, :, :], uu[:, :, :], bc(ones[:, 0:BLK].unsqueeze(1), [P, KT, BLK]),
                                ALU.add).then_inc(S("pool_steps"), 1)
                pool.wait_ge(S("sig_done"), b_before + 1)
                g.tensor_tensor(sg[:, :, :], sg[:, :, :], gg[:, :, :], ALU.mult).then_inc(S("pool_steps"), 1)
                pool.wait_ge(S("pool_steps"), at + 2)
                g.tensor_tensor(uu[:, :, :], uu[:, :, :], sg[:, :, :], ALU.mult).then_inc(S("glu_done"), 1)

            def store(b_before):
                pool.wait_ge(S("orow_ready"), b_before + 1)
                g.dma_start(rows_scratch[bass.ds(b_before * BLK, BLK), :], orow[:, :]).then_inc(S("rows_stored"), 16)

            row_in_block(0, 0, 0)
            g.tensor_copy(bcur[:, :], bgu[:, :, 0]).then_inc(S("bcur_ready"), 1)
            pool.wait_ge(S("oneh_ready"), 1)
            row_in_block(1, 1, 1)
            with pool.Fori(1, nblk) as b:
                glu(b - 1, PER * b - 1)
                e = expert_of(b)
                g.tensor_copy(bcur[:, :], bgu[:, :, bass.ds(e, 1)].rearrange("p f e -> p (f e)")).then_inc(
                    S("bcur_ready"), 1)
                e2 = expert_of(b + 1)
                pool.wait_ge(S("oneh_ready"), b + 1)
                row_in_block(b + 1, e2, PER * b + 1)
                store(b - 1)
            glu(nblk - 1, PER * nblk - 1)
            store(nblk - 1)

            pool.wait_ge(S("rows_stored"), 16 * nblk + 16)
            own.then(g.tensor_tensor(blkbase[:, :], blkbase[:, :], step64[:, :], ALU.subtract))
            for n in range(3 * TOPK):
                t, j = divmod(n, TOPK)
                r = P if t < 2 else TS
                if n >= 5:
                    pool.wait_ge(S("summed"), n - 5 + 1)
                dst = xres[0:r, n % 5, :] if n % 5 < 3 else hcopy[0:r, (n % 5 - 3) * D:(n % 5 - 2) * D]
                g.indirect_dma_start(dst, None, rows_scratch[:, :], bass.IndirectOffsetOnAxis(
                    ap=slotu[0:r, t, j:j + 1], axis=0)).then_inc(S(f"gathered{n % 5}"), 16)
            pool.wait_ge(S("copies_out"), 16 * (3 * TS + 2))

        @block.scalar
        def _(act):
            a = nc.scalar
            own = Chain(act, "act_chain")

            act.dma_start(x_tok[:, 0:2, :], x_prompt[0].rearrange("(t p) d -> p t d", p=P)).then_inc(S("x_in"), 16)
            act.dma_start(x_tok[0:TS, 2, :], x_sample.rearrange("b s d -> (b s) d")).then_inc(S("x_in"), 16)
            act.dma_start(wdt[:, :, :], w_in_v[:, :, DT_COL:DT_COL + HEADS]).then_inc(S("wdt_in"), 16)
            for k in range(KT):
                act.wait_ge(S("xT_psum"), k + 1)
                a.activation(xh[:, k, :], bank[k][:, 0:T], ACT.Copy).then_inc(S("xh_done"), 1)
                a.activation(xT[:, k, :], bank[k][:, 0:T], ACT.Copy).then_inc(S("xT_done"), 1)
            act_high(act, 0)
            act_high(act, 1)
            act.wait_ge(*reached("params_psum"))
            for i in range(2):
                a.activation(cs[:, 12 * i:12 * i + 12, 0:29], bank[i][:, 0:12 * 32].rearrange(
                    "p (f c) -> p f c", c=32)[:, :, 0:29], ACT.Copy).then_inc(S("params_ready"), 1)
            a.activation(bgu[:, :, :], bank[2].rearrange("p (f e) -> p f e", e=NE), ACT.Copy).then_inc(
                S("params_ready"), 1)
            a.activation(gn[:, :], bank[3][:, 0:ZT], ACT.Copy).then_inc(S("params_ready"), 1)
            act.wait_ge(*reached("dt_abs"))
            own.then(a.activation(dts[:, 1, :], dts[:, 1, :], ACT.Exp))
            a.activation(dts[:, 1, :], dts[:, 1, :], ACT.Ln, bias=1.0).then_inc(S("dt_ln"), 1)
            a.activation(hcol[:, 2:3], hcol[:, 1:2], ACT.Exp).then_inc(S("dt_ln"), 1)
            act.wait_ge(*reached("acum_ready"))
            a.activation(dts[:, 4, 0:TP], dts[:, 4, 0:TP], ACT.Exp, scale=-1.0).then_inc(S("dt_exp"), 1)
            a.activation(hcol[:, 4:5], acum[:, 1, P - 1:P], ACT.Exp).then_inc(S("dt_exp"), 1)
            a.activation(dts[:, 7, 8:16], dts[:, 3, TP:T], ACT.Exp).then_inc(S("dt_exp"), 1)

            def evacuate(c, m, rep, per, odd):
                act.wait_ge(S("tile_done"), m + 1)
                a.activation(proj[:, bass.ds(m, 1), :].rearrange("p a t -> p (a t)"),
                             bank[4 + (2 * c + odd) % 4][:, 0:T], ACT.Copy).then_inc(S("bank_free"), 1)

            def project(c, m, rep, per):
                evacuate(c, m, rep, per, 0)
                if c + 2 < N_PROJ:
                    act_high(act, c + 2, rep, per)
                evacuate(c, m + 1, rep, per, 1)

            with act.Fori(0, L1) as i:
                for j in range(RING):
                    project(j, 2 * j + 2 * RING * i, i, RING)
            act.wait_ge(*reached("dt_psum"))
            a.activation(dtok[:, :, :], bank[0][:, 0:6 * HEADS].rearrange("p (a h) -> p a h", a=6), ACT.Copy).then_inc(
                S("dtok_ready"), 1)
            a.activation(feat[:, :, :], bank[1][:, 0:ZT * 17].rearrange("p (a h) -> p a h", a=ZT), ACT.Copy).then_inc(
                S("dtok_ready"), 1)
            a.activation(dec1[:, :], bank[2][:, 0:HEADS], ACT.Copy).then_inc(S("dtok_ready"), 1)
            for c in range(L1 * RING, RUN1):
                project(c, 2 * c, 0, 0)
            for half in range(2):
                act.wait_ge(S("tail_psum"), half + 1)
                a.activation(tail[:, 12 * half:12 * half + 12, :],
                             psum[0:11, 0:3, :].rearrange("p b (f c) -> p (b f) c", c=P), ACT.Copy).then_inc(
                    S("tail_ready"), 1)
            act.wait_ge(S("tail_ready"), 2)
            act.dma_start(prompt_conv[0, 0].rearrange("j (f c) -> j f c", c=P), tail[0:3, :, :]).then_inc(
                S("conv_out"), 16)
            act.dma_start(sample_conv[0, :, 2, :].rearrange("b (f c) -> b f c", c=P), tail[3:11, :, :]).then_inc(
                S("conv_out"), 16)
            act.dma_start(sample_conv[0, :, 0:2, :], state_conv[0, :, 1:3, :]).then_inc(S("conv_out"), 16)
            with act.Fori(0, L2) as i:
                for j in range(RING):
                    c = RUN1 + j
                    project(c, 2 * c + 2 * RING * i, i, RING)
                    act.wait_ge(S("ctmp_done"), j + 1 + RING * i)
                    a.activation(csig[:, :, :], ctmp[:, :, :], ACT.Sigmoid).then_inc(S("csig_done"), 1)
            zstep = 0
            for c in range(RUN1 + L2 * RING, N_PROJ):
                project(c, 2 * c, 0, 0)
                for _ in range(2 if zstep < ZT // 2 else 0):
                    if zstep < 2:
                        act.wait_ge(S("conv_done"), 13)
                    else:
                        act.wait_ge(S("z_done"), zstep - 1)
                    a.activation((ctmp, csig)[zstep % 2][:, :, :], proj[:, 2 * zstep:2 * zstep + 2, :],
                                 ACT.Sigmoid).then_inc(S("zsig_done"), 1)
                    zstep += 1
            act.wait_ge(S("bank_free"), 4 + NT)
            for half in range(2):
                gt = proj[:, G0 + KT * half:G0 + KT * half + KT, :]
                a.activation(gt, gt, ACT.Sigmoid).then_inc(S("gates_ready"), 1)

            def ssd_prepare(it):
                c, gi = divmod(it, GROUPS)
                if it == 0:
                    act.wait_ge(S("z_done"), 8)
                    act.wait_ge(S("conv_out"), 48)
                act.wait_ge(S("ssd_prep"), it + 1)
                if it >= 2:
                    act.wait_ge(S("ssd_state"), it - 1)
                a.activation(btok[:, it % 2, :], bank[1][:, 0:P], ACT.Copy).then_inc(S("btok_ready"), 1)
                if c == 1:
                    if gi >= 2:
                        act.wait_ge(S("ssd_y"), it - 1)
                    a.activation(ctile[:, gi % 2, :, :], psum[:, 2:4, :].rearrange("p b (h l) -> p (b h) l", l=P),
                                 ACT.Exp).then_inc(S("cexp_done"), 1)
                act.wait_ge(S("larg_ready"), it + 1)
                a.activation(lmat[:, it % 2, :, :], lmat[:, it % 2, :, :], ACT.Exp).then_inc(S("lexp_done"), 1)

            def state_out(gi):
                act.wait_ge(S("hturn_psum"), gi + 1)
                if gi:
                    act.wait_ge(S("pssm_out"), 16 * gi)
                a.activation(hout[:, :, :], bank[6].rearrange("p (i n) -> p i n", n=P), ACT.Copy).then_inc(
                    S("hout_ready"), 1)
                act.wait_ge(S("hout_ready"), gi + 1)
                act.dma_start(prompt_ssm[0, 0, gi * HPG:(gi + 1) * HPG].rearrange("(i q) p n -> (q p) i n", q=2),
                              hout[:, :, :]).then_inc(S("pssm_out"), 16)

            for it in range(2 * GROUPS + 1):
                if it < 2 * GROUPS:
                    ssd_prepare(it)
                if 0 < it <= GROUPS:
                    act.wait_ge(S("ssd_state"), it)
                    a.activation(s0[:, (it - 1) * 512:it * 512], bank[5], ACT.Copy).then_inc(S("s0_ready"), 1)
                if it > GROUPS + 1:
                    state_out(it - GROUPS - 2)
            state_out(GROUPS - 1)

            def state_dram(t, b):
                return t[0, b].rearrange("(i q) p n -> (q p) i n", q=2)

            act.wait_ge(S("pssm_out"), 16 * GROUPS)
            act.wait_ge(S("y_done"), 2 * GROUPS)
            for b in range(HSN):
                act.dma_start(hs[:, b, :, :], state_dram(state_ssm, b)).then_inc(S(f"hs_in{b}"), 16)
            for b in range(TS):
                act.wait_ge(S("hnew_ready"), b + 1)
                act.dma_start(state_dram(sample_ssm, b), hs[:, b % HSN, :, :]).then_inc(S(f"hs_out{b % HSN}"), 16)
                if b and b + 2 < TS:
                    act.wait_ge(S("hs_read"), b)
                    act.wait_ge(S(f"hs_out{(b - 1) % HSN}"), 16 * ((b - 1) // HSN + 1))
                    act.dma_start(hs[:, (b + 2) % HSN, :, :], state_dram(state_ssm, b + 2)).then_inc(
                        S(f"hs_in{(b + 2) % HSN}"), 16)
            for b in range(HSN):
                act.wait_ge(S(f"hs_out{b}"), 16 * len(range(b, TS, HSN)))

            act.wait_ge(*reached("ys_done"))
            for gi in range(GROUPS):
                a.activation(ysq[:, 4 * gi:4 * gi + 4, :], proj[:, 4 * gi:4 * gi + 4, :], ACT.Square).then_inc(
                    S("ysq_ready"), 1)
            for gi in range(GROUPS):
                act.wait_ge(S("var_ready"), gi + 1)
                a.activation(rstd[:, gi, :], rstd[:, gi, :], ACT.Sqrt).then_inc(S("std_done"), 1)

            act.wait_ge(*reached("norm_done"))
            for t in range(2):
                act.wait_ge(S("kv_psum"), t + 1)
                a.activation(kvtok[:, t, :, :], psum[:, 3 * t:3 * t + 3, :].rearrange("p b (f c) -> p (b f) c", c=P),
                             ACT.Copy).then_inc(S("kvtok_ready"), 1)
            act.wait_ge(*reached("qkvs_psum"))
            a.activation(qkvs[:, 0:16, :], psum[0:TS, 0:4, :].rearrange("p b (f c) -> p (b f) c", c=P),
                         ACT.Copy).then_inc(S("qkvs_ready"), 1)
            a.activation(qkvs[:, 16:18, :], bank[4][0:TS, 0:2 * P].rearrange("p (f c) -> p f c", c=P),
                         ACT.Copy).then_inc(S("qkvs_ready"), 1)
            act.wait_ge(S("kvtok_ready"), 2)
            act.wait_ge(S("qkvs_ready"), 2)
            act.dma_start(q_scratch, qkvs[:, 0:6, :].rearrange("b f c -> b (f c)")).then_inc(S("q_out"), 16)
            for gi, (w, _) in enumerate(DIL):
                for kv in range(2):
                    f = 6 * kv + 2 * gi
                    if w == P:
                        act.dma_start(prompt_kv[gi][0, 0, :, kv].rearrange("t h e -> t (h e)"),
                                      kvtok[:, 1, f:f + 2, :].rearrange("p f c -> p (f c)")).then_inc(S("kv_out"), 16)
                    else:
                        act.dma_start(prompt_kv[gi][0, 0, w - TP:w, kv].rearrange("(t p) h e -> p t (h e)", p=P),
                                      kvtok[:, :, f:f + 2, :].rearrange("p t f c -> p t (f c)")).then_inc(
                            S("kv_out"), 16)
                    act.dma_start(sample_kv[gi][0, :, w - 1, kv].rearrange("b h e -> b (h e)"),
                                  qkvs[:, 6 + f:8 + f, :].rearrange("b f c -> b (f c)")).then_inc(S("kv_out"), 16)
            for h in range(NH):
                act.wait_ge(S("amax_ready"), h + 1)
                a.activation(pa[:, h, 0:P], pa[:, h, 0:P], ACT.Exp, bias=ast[:, 1, 0, h:h + 1],
                             accum_out=ast[:, 2, 0, h:h + 1])
                a.activation(pa[:, h, P:3 * P], pa[:, h, P:3 * P], ACT.Exp, bias=ast[:, 1, 1, h:h + 1],
                             accum_out=ast[:, 2, 1, h:h + 1]).then_inc(S("aexp_done"), 1)

            def cached(gi, kv):
                w, d = DIL[gi]
                n = min(P, PAST // d)
                v = caches[gi][0].rearrange("b (j d) t h e -> j b d t (h e)", d=d)
                return n, v[P - n:P, :, 0, kv, :]

            def load_keys(gi):
                n, kc = cached(gi, 0)
                act.dma_start(kq[gi][0:n, 0, :, :], kc).then_inc(S(f"keys_in{gi}"), 16)
                act.dma_start(kq[gi][0:n, 1, :, :], q_scratch[:, gi * 256:(gi + 1) * 256].unsqueeze(0).broadcast_to(
                    [n, TS, 256])).then_inc(S(f"keys_in{gi}"), 16)

            act.wait_ge(S("scores_psum"), NH)
            act.wait_ge(S("q_out"), 16)
            load_keys(0)
            act.wait_ge(S("aexp_done"), NH)
            a.activation(ast[:, 3, :, :], ast[:, 2, :, :], ACT.Ln).then_inc(stage("aln_done"), 1)
            act.wait_ge(*reached("adiff_ready"))
            a.activation(ast[:, 5, :, :], ast[:, 5, :, :], ACT.Exp).then_inc(stage("aw_done"), 1)
            for n in range(NH):
                act.wait_ge(S("pturn_psum"), n + 1)
                if n >= 2:
                    act.wait_ge(S("pv_done"), n - 1)
                a.activation(pT[:, n % 2, :], bank[n % 2][:, 0:3 * P], ACT.Copy).then_inc(S("pT_ready"), 1)

            act.wait_ge(S("pv_done"), NH)
            act.wait_ge(S("kv_out"), 16 * 12)
            load_keys(1)
            for gi in range(3):
                n, vc = cached(gi, 1)
                act.dma_start(vsel[0:n, gi, :, :], vc).then_inc(S("vsel_in"), 16)
            act.wait_ge(S("qk_done"), 1)
            load_keys(2)
            act.wait_ge(*reached("sarg_ready"))
            a.activation(ss[:, :, :], ss[:, :, :], ACT.Exp).then_inc(stage("sexp_done"), 1)
            act.wait_ge(*reached("ssum_ready"))
            a.activation(sst[:, 3, :], sst[:, 2, :], ACT.Ln).then_inc(stage("sln_done"), 1)
            act.wait_ge(*reached("sdiff_ready"))
            a.activation(sst[:, 5, :], sst[:, 5, :], ACT.Exp).then_inc(stage("sw_done"), 1)
            act.wait_ge(*reached("pj_psum"))
            for gi, (_, d) in enumerate(DIL):
                n = min(P, PAST // d)
                a.activation(pj[0:n, 4 * gi:4 * gi + 4, :], bank[3][0:n, 32 * gi:32 * gi + 32].rearrange(
                    "p (h b) -> p h b", b=TS), ACT.Copy).then_inc(S("pj_ready"), 1)
            act.wait_ge(*reached("so_psum"))
            a.activation(oT[:, :, TP:T], bank[4][:, 0:2 * TS].rearrange("p (f b) -> p f b", b=TS),
                         ACT.Copy).then_inc(stage("so_copied"), 1)

            act.wait_ge(S("merge_done"), KT)
            act.dma_start(xres[:, 0:2, :], x_prompt[0].rearrange("(t p) d -> p t d", p=P)).then_inc(S("xres_in"), 16)
            act.dma_start(xres[0:TS, 2, :], x_sample.rearrange("b s d -> (b s) d")).then_inc(S("xres_in"), 16)
            act.dma_start(lnp[:, 0, :], ln1_g.broadcast_to([P, D])).then_inc(S("xres_in"), 16)
            act.dma_start(lnp[:, 1, :], ln1_b.broadcast_to([P, D])).then_inc(S("xres_in"), 16)
            act.dma_start(wr[:, :, :], w_router[0].rearrange("(k p) e -> p k e", p=P)).then_inc(S("router_in"), 16)
            act.dma_start(br[:, :], b_router.broadcast_to([P, NE])).then_inc(S("router_in"), 16)
            act.dma_start(bdn[:, :], b_down[0]).then_inc(S("router_in"), 16)
            def deviation(t, nth):
                r = P if t < 2 else TS
                act.wait_ge(S("var_ready"), GROUPS + nth + 1)
                a.activation(lnst[0:r, t, 14:15], lnst[0:r, t, 14:15], ACT.Sqrt).then_inc(S("std_done"), 1)

            for t in range(3):
                deviation(t, t)
            act.wait_ge(*reached("x1_ready"))
            a.activation(x1h[:, :, :], x1[:, :, :], ACT.Copy).then_inc(stage("x1h_done"), 1)
            act.dma_start(lnp[:, 0, :], ln2_g.broadcast_to([P, D])).then_inc(S("ln2_in"), 16)
            act.dma_start(lnp[:, 1, :], ln2_b.broadcast_to([P, D])).then_inc(S("ln2_in"), 16)
            for k in range(KT):
                act.wait_ge(S("x1T_psum"), k + 1)
                a.activation(x1T[:, k, :], bank[k][:, 0:T], ACT.Copy).then_inc(S("x1T_ready"), 1)
            act.wait_ge(*reached("gdiff_ready"))
            a.activation(gate[:, :, :], gate[:, :, :], ACT.Exp).then_inc(stage("gexp_done"), 1)
            act.wait_ge(*reached("gmT_psum"))
            a.activation(gmT[:, :], bank[1][0:NE, 0:T], ACT.Copy).then_inc(stage("gmT_ready"), 1)

            for c in range(4, 4 + HL):
                act_high(act, STEP0 + c)
            act.wait_ge(*reached("table_ready"))
            nblk = act.value_load(tab[0:1, MAX_BLK + 3:MAX_BLK + 4], min_val=NE, max_val=MAX_BLK)

            def rows_high(n):
                act.wait_ge(S("gath_done"), n + 1)
                a.activation(xst[:, :, 0:BLK], bank[6].rearrange("p (k r) -> p k r", r=BLK), ACT.Copy).then_inc(
                    S("xst_high"), 1)

            def hidden_copy(n):
                act.wait_ge(S("split_used"), gate_up_used(n))
                a.activation(hcopy[:, :], psum[:, 0:4, :].rearrange("p b c -> p (b c)"), ACT.Copy).then_inc(
                    S("hcopy_done"), 1)

            def sigmoid(n):
                act.wait_ge(S("gate_in"), n + 1)
                a.activation(sg[:, :, :], gg[:, :, :], ACT.Sigmoid, scale=SW_ALPHA).then_inc(S("sig_done"), 1)

            def hidden_high(n):
                act.wait_ge(S("glu_done"), n + 1)
                a.activation(hst[:, :, 0:BLK], uu[:, :, :], ACT.Copy).then_inc(S("hst_high"), 1)

            def low_half(n, used):
                act.wait_ge(S("split_used"), used)
                act.wait_ge(S("low_read"), n + 1)
                a.activation(low[:, :], psum[BLK:P, 4:6, :].rearrange("p b c -> p (b c)"), ACT.Copy).then_inc(
                    S("low_copied"), 1)

            rows_high(0)
            for c in range(4 + HL, 15):
                act_high(act, STEP0 + c)
            hidden_copy(0)
            act_high(act, STEP0 + 15)
            rows_high(1)
            with act.Fori(1, nblk) as b:
                sigmoid(b - 1)
                for c in range(4, 6):
                    act_high(act, STEP0 + c, b, 12)
                hidden_high(b - 1)
                for c in range(6, 11):
                    act_high(act, STEP0 + c, b, 12)
                hidden_copy(b)
                act_high(act, STEP0 + 11, b, 12)
                rows_high(b + 1)
                for c in range(12, 15):
                    act_high(act, STEP0 + c, b, 12)
                low_half(b - 1, used(STEP0 + 11, b))
                act_high(act, STEP0 + 15, b, 12)
            sigmoid(nblk - 1)
            hidden_high(nblk - 1)
            low_half(nblk - 1, used(STEP0 + 3, nblk))
            for t in range(3):
                deviation(t, 3 + t)
                act.wait_ge(S("y_ready"), t + 1)
                if t < 2:
                    act.dma_start(y_prompt[0, t * P:(t + 1) * P, :], x1[:, t, :]).then_inc(S("y_out"), 16)
                else:
                    act.dma_start(y_sample.rearrange("b s d -> (b s) d"), x1[0:TS, 2, :]).then_inc(S("y_out"), 16)
            act.wait_ge(S("y_out"), 48)

        @block.vector
        def _(dve):
            v = nc.vector
            own = Chain(dve, "dve_chain")

            for k in range(KT):
                dve.wait_ge(S("xT_done"), k + 1)
                v.tensor_tensor(xl[:, k, :], xT[:, k, :], xh[:, k, :].bitcast(F32), ALU.subtract).then_inc(
                    S("xl_done"), 1)
            dve_low(dve, 0)
            dve_low(dve, 1)
            dve.wait_ge(S("ones_ready"), 1)
            dve.wait_ge(S("cols_in"), 48)
            dve.wait_ge(*reached("dt_raw"))
            own.then(v.tensor_scalar(dts[:, 0, :], bank[4][0:HEADS, 0:T], hcol[:, 0:1], None, ALU.add))
            v.scalar_tensor_tensor(out=dts[:, 1, :], in0=dts[:, 0, :], scalar=-1.0, in1=dts[:, 0, :], op0=ALU.mult,
                                   op1=ALU.min).then_inc(stage("dt_abs"), 1)
            dve.wait_ge(S("dt_ln"), 2)
            own.then(v.scalar_tensor_tensor(out=dts[:, 2, :], in0=dts[:, 0, :], scalar=0.0, in1=dts[:, 1, :],
                                            op0=ALU.max, op1=ALU.add))
            own.then(v.tensor_scalar(dts[:, 3, :], dts[:, 2, :], hcol[:, 2:3], -1.0, ALU.mult, ALU.mult))
            for c in range(2):
                own.then(v.tensor_tensor_scan(acum[:, c, :], ones[0:HEADS, :], dts[:, 3, c * P:(c + 1) * P], 0.0,
                                              ALU.mult, ALU.add))
            for c in range(2):
                last = v.tensor_scalar(dts[:, 4, c * P:(c + 1) * P], acum[:, c, :], acum[:, c, P - 1:P], None,
                                       ALU.subtract)
            last.then_inc(stage("acum_ready"), 1)
            v.tensor_copy(dts[:, 7, 0:8], dts[:, 2, TP:T]).then_inc(S("dt_ready"), 1)
            v.tensor_copy(dts[:, 7, 16:17], hcol[:, 3:4]).then_inc(S("dt_ready"), 1)
            dve.wait_ge(S("dt_exp"), 3)
            v.tensor_tensor(dts[:, 5, 0:TP], dts[:, 4, 0:TP], dts[:, 2, 0:TP], ALU.mult).then_inc(S("dt_ready"), 1)
            v.tensor_scalar(dts[:, 6, 0:HEADS], ident[0:HEADS, 0:HEADS], hcol[:, 4:5], None, ALU.mult).then_inc(
                S("dt_ready"), 1)

            with dve.Fori(0, L1) as i:
                for j in range(RING):
                    dve_low(dve, j + 2, i, RING)
            for c in range(L1 * RING + 2, RUN1 + 2):
                dve_low(dve, c)

            def convolve(f, n, steps):
                x = proj[:, bass.ds(f + X0, 2), :]
                w = cs[:, bass.ds(f, 2), :]
                dve.wait_ge(S("conv_done"), n + 1)
                for k in range(2):
                    last = v.tensor_scalar(ctmp[:, k, :], x[:, k, :], w[:, k, 3:4], w[:, k, 4:5], ALU.mult, ALU.add)
                last.then_inc(S("conv_steps"), 1)
                for m in range(1, CW):
                    dve.wait_ge(S("conv_steps"), steps + m)
                    for k in range(2):
                        wk = w[:, k, 3 - m:4 - m]
                        v.scalar_tensor_tensor(out=ctmp[:, k, m:TP], in0=x[:, k, 0:TP - m], scalar=wk,
                                               in1=ctmp[:, k, m:TP], op0=ALU.mult, op1=ALU.add)
                        st = w[:, k, 5:29].rearrange("p (b j) -> p b j", j=3)[:, :, 3 - m]
                        last = v.scalar_tensor_tensor(out=ctmp[:, k, TP:T], in0=st, scalar=wk, in1=ctmp[:, k, TP:T],
                                                      op0=ALU.mult, op1=ALU.add)
                    last.then_inc(S("conv_steps" if m < 3 else "ctmp_done"), 1)

            dve.wait_ge(S("params_ready"), 4)
            dve.wait_ge(S("tail_psum"), 2)
            dve.wait_ge(S("bank_free"), 4 + ZT + XT)
            with dve.Fori(0, L2) as i:
                for j in range(RING):
                    convolve(2 * j + 2 * RING * i, j + RING * i, 3 * j + 3 * RING * i)
                    dve_low(dve, RUN1 + j + 2, i, RING)
            step = 0
            for c in range(RUN1 + L2 * RING + 2, N_PROJ + 2):
                if c < N_PROJ:
                    dve_low(dve, c)
                for _ in range(2):
                    if step < ZT // 2:
                        z = proj[:, 2 * step:2 * step + 2, :]
                        dve.wait_ge(S("zsig_done"), step + 1)
                        v.tensor_tensor(z, z, (ctmp, csig)[step % 2][:, :, :], ALU.mult).then_inc(S("z_done"), 1)
                        step += 1

            dve.wait_ge(S("dtok_ready"), 3)
            dve.wait_ge(S("conv_done"), 13)
            dve.wait_ge(S("z_done"), ZT // 2)
            dve.wait_ge(S("conv_out"), 48)

            def per_head(ap, n):
                return bc(ap.unsqueeze(2), [P, HPG, n])

            def ssd_prepare(it):
                c, gi = divmod(it, GROUPS)
                heads = slice(gi * HPG, (gi + 1) * HPG)
                dve.wait_ge(S("ssd_prep"), it + 1)
                if it >= 2:
                    dve.wait_ge(S("ssd_state"), it - 1)
                if c == 1:
                    dve.wait_ge(S("cexp_done"), gi + 1)
                lm = lmat[:, it % 2, :, :]
                own.then(v.tensor_tensor(lm, psum[:, 2:4, :].rearrange("p b (h l) -> p (b h) l", l=P),
                                         per_head(dtok[:, 2 + c, heads], P), ALU.subtract))
                v.tensor_scalar(lm, lm, 0.0, None, ALU.min).then_inc(S("larg_ready"), 1)
                x = bank[0].rearrange("p (h e) -> p h e", e=HP)
                v.tensor_tensor(xdt[:, it % 2, :].rearrange("p (h e) -> p h e", e=HP), x,
                                per_head(dtok[:, c, heads], HP), ALU.mult)
                v.tensor_tensor(xw[:, it % 2, :].rearrange("p (h e) -> p h e", e=HP), x,
                                per_head(dtok[:, 4 + c, heads], HP), ALU.mult)
                dve.wait_ge(S("btok_ready"), it + 1)
                own.then(v.tensor_tensor(cbm[:, it % 2, :], bank[1][:, P:2 * P], later[:, :], ALU.mult))
                dve.wait_ge(S("lexp_done"), it + 1)
                v.tensor_tensor(lm, lm, bc(cbm[:, it % 2, :].unsqueeze(1), [P, HPG, P]), ALU.mult).then_inc(
                    S("scores_ready"), 1)

            def ssd_finish(it):
                c, gi = divmod(it, GROUPS)
                cols = slice(c * P, (c + 1) * P)
                dve.wait_ge(S("ssd_y"), it + 1)
                for f in range(4):
                    last = v.scalar_tensor_tensor(out=yt[:, f * P:(f + 1) * P], in0=proj[:, X0 + 4 * gi + f, cols],
                                                  scalar=feat[:, 4 * gi + f, 16:17],
                                                  in1=bank[4][:, f * P:(f + 1) * P], op0=ALU.mult, op1=ALU.add)
                own.then(last)
                z = proj[:, 4 * gi:4 * gi + 4, cols]
                v.tensor_tensor(z, z, yt[:, :].rearrange("p (f l) -> p f l", l=P), ALU.mult).then_inc(S("y_done"), 1)
                if c == 1:
                    if gi:
                        dve.wait_ge(S("hturn_psum"), gi)
                    h = hT[:, :].rearrange("p (h e) -> p h e", e=HP)
                    own.then(v.tensor_tensor(h, s0[:, gi * 512:(gi + 1) * 512].rearrange("p (h e) -> p h e", e=HP),
                                             per_head(dec1[:, gi * HPG:(gi + 1) * HPG], HP), ALU.mult))
                    dve.wait_ge(S("ssd_state"), it + 1)
                    v.tensor_tensor(hT[:, :], hT[:, :], bank[5], ALU.add).then_inc(S("hT_ready"), 1)

            ssd_prepare(0)
            for it in range(2 * GROUPS):
                if it + 1 < 2 * GROUPS:
                    ssd_prepare(it + 1)
                ssd_finish(it)

            dve.wait_ge(S("pssm_out"), 16 * GROUPS)
            xs_ = proj[:, X0:X0 + ZT, TP:T]
            v.tensor_tensor(xdts[:, :, :], xs_, feat[:, :, 0:TS], ALU.mult)
            own.then(v.tensor_tensor(xskip[:, :, :], xs_, bc(feat[:, :, 16:17], [P, ZT, TS]), ALU.mult))

            def spread(bk):
                return bc(bank[bk].rearrange("p (g n) -> p g n", n=P).unsqueeze(2), [P, GROUPS, 4, P])

            def grouped(ap):
                return ap.rearrange("p (g f) n -> p g f n", g=GROUPS)

            def times_b(b):
                dve.wait_ge(S("bc_psum"), b + 1)
                if b >= 2:
                    dve.wait_ge(S("hs_read"), b - 1)
                v.tensor_tensor(grouped(sprod[:, b % 2, :, :]), spread(2 * (b % 2)),
                                bc(grouped(xdts[:, :, b:b + 1]), [P, GROUPS, 4, P]), ALU.mult).then_inc(
                    S("bx_ready"), 1)

            times_b(0)
            for b in range(TS):
                if b + 1 < TS:
                    times_b(b + 1)
                dve.wait_ge(S("hnew_ready"), b + 1)
                own.then(v.tensor_tensor(grouped(sprod[:, b % 2, :, :]), grouped(hs[:, b % HSN, :, :]),
                                         spread(2 * (b % 2) + 1), ALU.mult))
                v.tensor_reduce(ysum[:, :, b:b + 1], sprod[:, b % 2, :, :], X, ALU.add).then_inc(S("hs_read"), 1)
            dve.wait_ge(S("hs_read"), TS)
            own.then(v.tensor_tensor(ysum[:, :, :], ysum[:, :, :], xskip[:, :, :], ALU.add))
            zs = proj[:, 0:ZT, TP:T]
            v.tensor_tensor(zs, zs, ysum[:, :, :], ALU.mult).then_inc(stage("ys_done"), 1)

            for gi in range(GROUPS):
                dve.wait_ge(S("ss_psum"), gi + 1)
                v.tensor_scalar(rstd[:, gi, :], bank[gi][:, 0:T], 1.0 / 512, EPS, ALU.mult, ALU.add).then_inc(
                    S("var_ready"), 1)
                dve.wait_ge(S("std_done"), gi + 1)
                own.then(v.reciprocal(rstd[:, gi, :], rstd[:, gi, :]))
                for f in range(4 * gi, 4 * gi + 4):
                    last = v.scalar_tensor_tensor(out=proj[:, f, :], in0=proj[:, f, :], scalar=gn[:, f:f + 1],
                                                  in1=rstd[:, gi, :], op0=ALU.mult, op1=ALU.mult)
            last.then_inc(stage("norm_done"), 1)

            dve.wait_ge(S("rel_ready"), 3)
            dve.wait_ge(*reached("norm_done"))
            own.then(v.tensor_copy(rel[:, :], reli))
            for gi, (w, d) in enumerate(DIL):
                mk = masks[:, gi, :]
                own.then(v.tensor_scalar(relb, reli, d - 1, None, ALU.bitwise_and))
                own.then(v.tensor_copy(mk, relb))
                own.then(v.tensor_scalar(mk, mk, 0.0, None, ALU.is_equal))
                own.then(v.scalar_tensor_tensor(out=mk, in0=rel[:, :], scalar=0.0, in1=mk, op0=ALU.is_ge, op1=ALU.mult))
                own.then(v.scalar_tensor_tensor(out=mk, in0=rel[:, :], scalar=float(w), in1=mk, op0=ALU.is_le,
                                                op1=ALU.mult))
                own.then(v.tensor_scalar(mk, mk, -1.0, -NEG, ALU.add, ALU.mult))
            for h in range(NH):
                bs = bias[:, h % 2, :]
                own.then(v.scalar_tensor_tensor(out=bs, in0=rel[:, :], scalar=-SLOPES[h], in1=masks[:, h // HG, :],
                                                op0=ALU.mult, op1=ALU.add))
                dve.wait_ge(S("scores_psum"), h + 1)
                v.scalar_tensor_tensor(out=pa[:, h, :], in0=bank[6 + h % 2][:, 0:3 * P], scalar=SCALE, in1=bs,
                                       op0=ALU.mult, op1=ALU.add).then_inc(S("score_read"), 1)
                dve.wait_ge(S("score_read"), h + 1)
                v.tensor_reduce(ast[:, 0, 0, h:h + 1], pa[:, h, 0:P], X, ALU.max)
                own.then(v.tensor_reduce(ast[:, 0, 1, h:h + 1], pa[:, h, P:3 * P], X, ALU.max))
                v.tensor_scalar(ast[:, 1, :, h:h + 1], ast[:, 0, :, h:h + 1], -1.0, None, ALU.mult).then_inc(
                    S("amax_ready"), 1)

            def merge_weights(st, n, dims, ready):
                def by_group(k):
                    return [st(k, gi) for gi in range(3)]
                dve.wait_ge(*reached(ready[0]))
                own.then(v.tensor_tensor(st(3), st(3), st(0), ALU.add))
                lse = by_group(3)
                own.then(v.tensor_tensor(st(4, 0), lse[0], lse[1], ALU.max))
                own.then(v.tensor_tensor(st(4, 0), st(4, 0), lse[2], ALU.max))
                for gi in range(3):
                    last = v.tensor_tensor(st(5, gi), lse[gi], st(4, 0), ALU.subtract)
                last.then_inc(stage(ready[1]), 1)
                dve.wait_ge(*reached(ready[2]))
                w = by_group(5)
                own.then(v.tensor_tensor(st(4, 1), w[0], w[1], ALU.add))
                own.then(v.tensor_tensor(st(4, 1), st(4, 1), w[2], ALU.add))
                for gi in range(3):
                    last = v.tensor_tensor(st(6, gi), st(2, gi), st(4, 1), ALU.mult)
                own.then(last)
                own.then(v.reciprocal(st(6), st(6)))

            def ast_of(k, gi=None):
                return ast[:, k, :, :] if gi is None else ast[:, k, :, gi * HG:(gi + 1) * HG]

            merge_weights(ast_of, P, 2, ("aln_done", "adiff_ready", "aw_done"))
            v.tensor_tensor(ast_of(7), ast_of(5), ast_of(6), ALU.mult).then_inc(stage("coef_ready"), 1)
            dve.wait_ge(S("pv_done"), NH)
            for t in range(2):
                v.tensor_copy(oT[:, :, t * P:(t + 1) * P],
                              bank[2 + t][:, 0:2 * P].rearrange("p (f i) -> p f i", f=2)).then_inc(S("oT_ready"), 1)

            keys = [min(P, PAST // d) for _, d in DIL]
            dve.wait_ge(S("rel_ready"), 4)
            for gi, (w, d) in enumerate(DIL):
                n = keys[gi]
                keys_, q_ = kq[gi][0:n, 0, :, :], kq[gi][0:n, 1, :, :]
                dve.wait_ge(S(f"keys_in{gi}"), 32)
                own.then(v.tensor_tensor(q_, q_, keys_, ALU.mult))
                v.tensor_reduce(stok[0:n, gi * HG:(gi + 1) * HG, :].rearrange("p h b -> p b h"),
                                q_.rearrange("p b (h e) -> p b h e", e=DH), X, ALU.add).then_inc(
                    S("qk_done"), 1)
                for h in range(gi * HG, (gi + 1) * HG):
                    last = v.tensor_scalar(ss[:, h, 0:n], sback[:, P - n:P], -SLOPES[h] * d, None, ALU.mult)
                own.then(last)
            own.then(v.memset(ss[:, 2 * HG:NH, keys[2]:P], NEG))
            qs = qkvs[:, 0:6, :].rearrange("b f c -> b (f c)")
            ks = qkvs[:, 6:12, :].rearrange("b f c -> b (f c)")
            vs = qkvs[:, 12:18, :].rearrange("b f c -> b (f c)")
            own.then(v.tensor_tensor(selfo[:, :], qs, ks, ALU.mult))
            own.then(v.tensor_reduce(ss[:, :, P:P + 1], selfo[:, :].rearrange("b (h e) -> b h e", e=DH), X, ALU.add))
            own.then(v.tensor_scalar(ss[:, :, P:P + 1], ss[:, :, P:P + 1], SCALE, None, ALU.mult))
            dve.wait_ge(*reached("sturn_psum"))
            for gi in range(3):
                n = keys[gi]
                part = ss[:, gi * HG:(gi + 1) * HG, 0:n]
                last = v.scalar_tensor_tensor(out=part, in0=bank[gi][0:TS, :].rearrange("b (h j) -> b h j", j=P)[:, :, 0:n],
                                              scalar=SCALE, in1=part, op0=ALU.mult, op1=ALU.add)
            own.then(last)
            own.then(v.tensor_reduce(sst[:, 0, :], ss[:, :, :], X, ALU.max))
            v.tensor_tensor(ss[:, :, :], ss[:, :, :], bc(sst[:, 0, :].unsqueeze(2), [TS, NH, P + 1]),
                            ALU.subtract).then_inc(stage("sarg_ready"), 1)
            dve.wait_ge(*reached("sexp_done"))
            v.tensor_reduce(sst[:, 2, :], ss[:, :, :], X, ALU.add).then_inc(stage("ssum_ready"), 1)

            def sst_of(k, gi=None):
                return sst[:, k, :] if gi is None else sst[:, k, gi * HG:(gi + 1) * HG]

            merge_weights(sst_of, TS, 1, ("sln_done", "sdiff_ready", "sw_done"))
            own.then(v.tensor_tensor(sst_of(7), sst_of(5), sst_of(6), ALU.mult))
            own.then(v.tensor_tensor(ss[:, :, :], ss[:, :, :], bc(sst[:, 7, :].unsqueeze(2), [TS, NH, P + 1]), ALU.mult))
            v.tensor_copy(sst[:, 1, :], sst[:, 7, :]).then_inc(stage("sp_ready"), 1)
            own.then(v.tensor_tensor(selfo[:, :].rearrange("b (h e) -> b h e", e=DH),
                                     vs.rearrange("b (h e) -> b h e", e=DH),
                                     bc(ss[:, :, P:P + 1], [TS, NH, DH]), ALU.mult))
            own.then(v.tensor_tensor(selfo[:, 0:256], selfo[:, 0:256], selfo[:, 256:512], ALU.add))
            v.tensor_tensor(selfo[:, 0:256], selfo[:, 0:256], selfo[:, 512:768], ALU.add).then_inc(stage("selfo_ready"), 1)
            dve.wait_ge(S("vsel_in"), 48)
            for gi in range(3):
                n = keys[gi]
                dve.wait_ge(S("pj_ready"), gi + 1)
                vv = vsel[0:n, gi, :, :].rearrange("p b (h e) -> p b h e", e=DH)
                pp = pj[0:n, gi * HG:(gi + 1) * HG, :].rearrange("p h b -> p b h").unsqueeze(3)
                v.tensor_tensor(vv, vv, bc(pp, [n, TS, HG, DH]), ALU.mult).then_inc(S("pvs_ready"), 1)
            dve.wait_ge(*reached("so_copied"))
            v.tensor_tensor(oT[:, :, TP:T], oT[:, :, TP:T], bank[5][:, 0:2 * TS].rearrange("p (f b) -> p f b", b=TS),
                            ALU.add).then_inc(S("oT_ready"), 1)

            for m in range(KT):
                dve.wait_ge(S("branch_a"), m + 1)
                if m == 0:
                    dve.wait_ge(S("gates_ready"), 2)
                v.tensor_tensor(merged[:, m, :], bank[m][:, 0:T], proj[:, G0 + m, :], ALU.mult).then_inc(
                    S("a_read"), 1)
            for m in range(KT):
                dve.wait_ge(S("branch_b"), m + 1)
                own.then(v.tensor_tensor(bpart[:, m, :], bank[m][:, 0:T], proj[:, G0 + KT + m, :], ALU.mult))
                v.tensor_tensor(merged[:, m, :], merged[:, m, :], bpart[:, m, :], ALU.add).then_inc(
                    S("merge_done"), 1)

            def layer_norm(t, scale, shift, nth):
                r = P if t < 2 else TS
                st = lnst[0:r, t, :]
                xs_ = x1[0:r, t, :]
                for half in range(2):
                    last = v.bn_stats(st[:, 6 * half:6 * half + 6], xs_[:, 512 * half:512 * half + 512])
                own.then(last)
                own.then(v.bn_aggr(st[:, 12:14], st[:, 0:12]))
                v.tensor_scalar(st[:, 14:15], st[:, 13:14], EPS, None, ALU.add).then_inc(S("var_ready"), 1)
                dve.wait_ge(S("std_done"), GROUPS + nth + 1)
                own.then(v.reciprocal(st[:, 14:15], st[:, 14:15]))
                own.then(v.tensor_scalar(xs_, xs_, st[:, 12:13], st[:, 14:15], ALU.subtract, ALU.mult))
                own.then(v.tensor_tensor(xs_, xs_, scale[0:r], ALU.mult))
                return v.tensor_tensor(xs_, xs_, shift[0:r], ALU.add)

            dve.wait_ge(S("xres_in"), 64)
            dve.wait_ge(S("merge_done"), KT)
            own.then(v.memset(x1[:, 2, :], 0.0))
            for t in range(3):
                r = P if t < 2 else TS
                dve.wait_ge(S("mix_psum"), t + 1)
                for half in range(2):
                    cols = slice(512 * half, 512 * half + 512)
                    last = v.scalar_tensor_tensor(out=x1[0:r, t, cols], in0=xres[0:r, t, cols], scalar=ALPHA,
                                                  in1=bank[2 * t + half][0:r, :], op0=ALU.mult, op1=ALU.add)
                own.then(last)
                own.then(layer_norm(t, lnp[:, 0, :], lnp[:, 1, :], t))
            v.tensor_copy(lnst[:, 0, 15:16], lnst[:, 0, 14:15]).then_inc(stage("x1_ready"), 1)
            dve.wait_ge(*reached("x1h_done"))
            v.tensor_tensor(x1l[:, :, :], x1[:, :, :], x1h[:, :, :].bitcast(F32), ALU.subtract).then_inc(stage("x1l_done"), 1)

            dve.wait_ge(S("router_in"), 48)
            dve.wait_ge(S("ecol_ready"), 3)
            for z in (lg, ixf, gate, pick, mask, slotj):
                last = v.memset(z[:], 0.0)
            own.then(last)
            own.then(v.memset(gsum[:], 1.0))
            own.then(v.memset(slot[:], -1.0))
            dve.wait_ge(*reached("logits_psum"))
            own.then(v.memset(mx[:], 0.0))
            for t in range(3):
                r = P if t < 2 else TS
                own.then(v.tensor_tensor(lg[0:r, t, :], bank[0][0:r, t * NE:(t + 1) * NE], br[0:r, :], ALU.add))
                own.then(v.max(mx[0:r, t, :], lg[0:r, t, :]))
                own.then(v.max_index(ix[0:r, t, :], mx[0:r, t, :], lg[0:r, t, :]))
                own.then(v.tensor_copy(ixf[0:r, t, :], ix[0:r, t, :]))
                own.then(v.tensor_scalar(gate[0:r, t, :], mx[0:r, t, 0:TOPK], mx[0:r, t, 0:1], None, ALU.subtract))
                for j in range(TOPK):
                    last = v.tensor_scalar(pick[0:r, t, j, :], ecol[0:r, :], ixf[0:r, t, j:j + 1], None, ALU.is_equal)
                own.then(last)
            v.tensor_reduce(mask[:, :, :], pick[:, :, :, :].rearrange("p t j e -> p t e j"), X, ALU.add).then_inc(stage("mask_ready"), 1)
            v.tensor_copy(gsum[:, 0:1], gsum[:, 0:1]).then_inc(stage("gdiff_ready"), 1)
            dve.wait_ge(*reached("gexp_done"))
            own.then(v.tensor_reduce(gsum[:, :], gate[:, :, :], X, ALU.add))
            own.then(v.reciprocal(gsum[:, :], gsum[:, :]))
            own.then(v.tensor_tensor(gate[:, :, :], gate[:, :, :], bc(gsum[:, :].unsqueeze(2), [P, 3, TOPK]), ALU.mult))
            own.then(v.tensor_tensor(pick2[:, :, :, :].rearrange("p t j e -> p (t j) e"),
                                     pick[:, :, :, :].rearrange("p t j e -> p (t j) e"),
                                     bc(gate[:, :, :].rearrange("p t j -> p (t j)").unsqueeze(2), [P, 3 * TOPK, NE]),
                                     ALU.mult))
            v.tensor_reduce(gm[:, :, :], pick2[:, :, :, :].rearrange("p t j e -> p t e j"), X, ALU.add).then_inc(stage("gm_ready"), 1)
            dve.wait_ge(*reached("rank_psum"))
            own.then(v.tensor_copy(rank[:, :, :], bank[2][:, 0:4 * NE].rearrange("p (t e) -> p t e", e=NE)))
            total = rank[:, 3, :]
            over_, incl, delta, zero_ = cnt[:, 0, :], cnt[:, 1, :], cnt[:, 2, :], cnt[:, 3, :]
            own.then(v.tensor_scalar(over_, total, float(BLK), None, ALU.is_gt))
            for m in range(2, 5):
                own.then(v.scalar_tensor_tensor(out=over_, in0=total, scalar=float(BLK * m), in1=over_, op0=ALU.is_gt,
                                                op1=ALU.add))
            own.then(v.memset(zero_, 1.0))
            own.then(v.tensor_tensor_scan(incl, zero_, over_, 0.0, ALU.mult, ALU.add))
            own.then(v.tensor_tensor(delta, incl, over_, ALU.subtract))
            own.then(v.tensor_tensor(delta, delta, ecol[:, :], ALU.subtract))
            own.then(v.tensor_scalar(delta, delta, float(NE - 1), float(BLK), ALU.add, ALU.mult))
            for t in range(3):
                own.then(v.scalar_tensor_tensor(out=slot[:, t, :], in0=rank[:, t, :], scalar=float(BLK), in1=delta,
                                                op0=ALU.is_ge, op1=ALU.mult))
                own.then(v.scalar_tensor_tensor(out=slot[:, t, :], in0=ecol[:, :], scalar=float(BLK), in1=slot[:, t, :],
                                                op0=ALU.mult, op1=ALU.add))
                own.then(v.tensor_tensor(slot[:, t, :], slot[:, t, :], rank[:, t, :], ALU.add))
            own.then(v.tensor_tensor(pick2[:, :, :, :], pick[:, :, :, :], bc(slot[:, :, :].unsqueeze(2),
                                                                          [P, 3, TOPK, NE]), ALU.mult))
            own.then(v.tensor_reduce(slotj[:, :, :], pick2[:, :, :, :], X, ALU.add))
            own.then(v.tensor_copy(slotu[:, :, :], slotj[:, :, :]))
            own.then(v.tensor_scalar(slot[:, :, :], slot[:, :, :], 1.0, None, ALU.add))
            own.then(v.tensor_tensor(slot[:, :, :], slot[:, :, :], mask[:, :, :], ALU.mult))
            own.then(v.tensor_scalar(slot[:, :, :], slot[:, :, :], -1.0, None, ALU.add))
            own.then(v.tensor_tensor(ovc[:, :, :], ovc[:, :, :], bc(incl[0:1, :].unsqueeze(1), [1, MAX_OV, NE]),
                                     ALU.is_ge))
            own.then(v.tensor_reduce(tabf[0:1, NE:MAX_BLK], ovc[:, :, :], X, ALU.add))
            own.then(v.tensor_scalar(tabf[0:1, NE:MAX_BLK + 2], tabf[0:1, NE:MAX_BLK + 2], float(NE - 1), None, ALU.min))
            own.then(v.tensor_scalar(tabf[0:1, MAX_BLK + 2:MAX_BLK + 3], incl[0:1, NE - 1:NE], 1.0, None, ALU.min))
            own.then(v.tensor_scalar(tabf[0:1, MAX_BLK + 3:MAX_BLK + 4], incl[0:1, NE - 1:NE], float(NE), None, ALU.add))
            v.tensor_copy(tab[:, :], tabf[:, :]).then_inc(stage("table_ready"), 1)
            dve.wait_ge(*reached("table_ready"))
            nblk = dve.value_load(tab[0:1, MAX_BLK + 3:MAX_BLK + 4], min_val=NE, max_val=MAX_BLK)

            def one_hot(n):
                dve.wait_ge(S("sl_ready"), n + 1)
                v.tensor_tensor(oneh[:, :, :], bc(iota64[:, :].unsqueeze(1), [P, 3, BLK]),
                                bc(sl[:, :].unsqueeze(2), [P, 3, BLK]), ALU.is_equal).then_inc(S("oneh_ready"), 1)

            def rows_low(n):
                dve.wait_ge(S("gath_done"), n + 1)
                v.tensor_copy(xst[:, :, BLK:P], bank[7].rearrange("p (k r) -> p k r", r=BLK)).then_inc(
                    S("xst_low"), 1)

            def add_bias(n):
                dve.wait_ge(S("ht_done"), n + 1)
                dve.wait_ge(S("bcur_ready"), n + 1)
                for half, dst in enumerate((gg, uu)):
                    b = bcur[:, half * KT:half * KT + KT].unsqueeze(2)
                    last = v.tensor_tensor(dst[:, :, :], bank[6 + half].rearrange("p (k r) -> p k r", r=BLK),
                                           bc(b, [P, KT, BLK]), ALU.add)
                last.then_inc(S("ht_read"), 1)
                dve.wait_ge(S("ht_read"), n + 1)
                v.tensor_scalar(gg[:, :, :], gg[:, :, :], LIMIT, None, ALU.min).then_inc(S("gate_in"), 1)
                v.tensor_scalar(uu[:, :, :], uu[:, :, :], LIMIT, -LIMIT, ALU.min, ALU.max).then_inc(S("up_in"), 1)

            def hidden_low(n):
                dve.wait_ge(S("hst_high"), n + 1)
                v.tensor_tensor(hst[:, :, BLK:P], uu[:, :, :], hst[:, :, 0:BLK].bitcast(F32), ALU.subtract).then_inc(
                    S("hst_low"), 1)

            def add_halves(n):
                dve.wait_ge(S("low_copied"), n + 1)
                dve.wait_ge(S("rows_stored"), 16 * n + 16)
                v.tensor_tensor(orow[:, :], psum[0:BLK, 4:6, :].rearrange("p b c -> p (b c)"), low[:, :],
                                ALU.add).then_inc(S("orow_ready"), 1)
                dve.wait_ge(S("orow_ready"), n + 1)
                v.tensor_copy(lnst[:, 0, 15:16], lnst[:, 0, 14:15]).then_inc(S("low_read"), 1)

            dve.wait_ge(S("consts_ready"), 3)
            one_hot(0)
            for c in range(4, 4 + HL):
                dve_low(dve, STEP0 + c)
            rows_low(0)
            one_hot(1)
            for c in range(4 + HL, 12):
                dve_low(dve, STEP0 + c)
            for t in range(3):
                r = P if t < 2 else TS
                dve.wait_ge(S("gb_psum"), t + 1)
                for half in range(2):
                    cols = slice(512 * half, 512 * half + 512)
                    last = v.scalar_tensor_tensor(out=x1[0:r, t, cols], in0=x1[0:r, t, cols], scalar=ALPHA,
                                                  in1=bank[4 + half][0:r, :], op0=ALU.mult, op1=ALU.add)
                last.then_inc(S("gb_read"), 1)
            for c in range(12, 16):
                dve_low(dve, STEP0 + c)
            rows_low(1)
            with dve.Fori(1, nblk) as b:
                add_bias(b - 1)
                for c in range(4, 6):
                    dve_low(dve, STEP0 + c, b, 12)
                hidden_low(b - 1)
                one_hot(b + 1)
                for c in range(6, 12):
                    dve_low(dve, STEP0 + c, b, 12)
                rows_low(b + 1)
                for c in range(12, 15):
                    dve_low(dve, STEP0 + c, b, 12)
                add_halves(b - 1)
                dve_low(dve, STEP0 + 15, b, 12)
            add_bias(nblk - 1)
            hidden_low(nblk - 1)
            add_halves(nblk - 1)

            dve.wait_ge(S("ln2_in"), 32)
            for n in range(3 * TOPK):
                t, j = divmod(n, TOPK)
                r = P if t < 2 else TS
                src = xres[0:r, n % 5, :] if n % 5 < 3 else hcopy[0:r, (n % 5 - 3) * D:(n % 5 - 2) * D]
                dve.wait_ge(S(f"gathered{n % 5}"), 16 * (n // 5 + 1))
                v.scalar_tensor_tensor(out=x1[0:r, t, :], in0=src, scalar=gate[0:r, t, j:j + 1], in1=x1[0:r, t, :],
                                       op0=ALU.mult, op1=ALU.add).then_inc(S("summed"), 1)
                dve.wait_ge(S("summed"), n + 1)
                if j == TOPK - 1:
                    layer_norm(t, lnp[:, 0, :], lnp[:, 1, :], 3 + t).then_inc(S("y_ready"), 1)

        @block.tensor
        def _(pe):
            mm = nc.tensor.matmul
            tr = nc.tensor.transpose

            pe.wait_ge(S("ident_ready"), 1)
            pe.wait_ge(S("x_in"), 32)
            for k in range(KT):
                for t in range(3):
                    r = P if t < 2 else TS
                    last = tr(bank[k][:, t * P:t * P + r], x_tok[0:r, t, k * P:(k + 1) * P], ident[0:r, 0:r])
                last.then_inc(S("xT_psum"), 1)
            pe.wait_ge(S("rows_in"), 80)
            pe.wait_ge(S("xl_done"), KT)
            pe.wait_ge(S("xT_done"), KT)
            for f in range(XT):
                i, o = divmod(f, 12)
                tr(bank[i][:, 32 * o:32 * o + 29], rows[:, f * P:(f + 1) * P], ident[0:29, 0:29])
            for f in range(2 * KT):
                tr(bank[2][:, NE * f:NE * f + NE], bgu_rows[:, f * P:(f + 1) * P], ident[0:NE, 0:NE])
            tr(bank[3][:, 0:ZT], gn_rows, ident[0:ZT, 0:ZT]).then_inc(stage("params_psum"), 1)
            pe.wait_ge(S("wdt_in"), 16)
            for k in range(KT):
                last = mm(bank[4][0:HEADS, 0:T], wdt[:, k, :], xT[:, k, :], start=(k == 0), stop=(k == KT - 1))
            last.then_inc(stage("dt_raw"), 1)
            pe.wait_ge(S("params_ready"), 4)
            pe.wait_ge(*reached("dt_abs"))

            def project(c, m, rep, per):
                hi, lo = pe_split(pe, c, rep, per)
                for odd in range(2):
                    out = bank[4 + (2 * c + odd) % 4][:, 0:T]
                    pe.wait_ge(S("bank_free"), m + odd + 1)
                    for k in range(KT):
                        cols = slice(k * 256 + odd * P, k * 256 + odd * P + P)
                        mm(out, hi[:, cols], xh[:, k, :], start=(k == 0), stop=False)
                        mm(out, hi[:, cols], xl[:, k, :], start=False, stop=False)
                        last = mm(out, lo[:, cols], xh[:, k, :], start=False, stop=(k == KT - 1))
                    last.then_inc(S("tile_done"), 1)

            with pe.Fori(0, L1) as i:
                for j in range(RING):
                    project(j, 2 * j + 2 * RING * i, i, RING)
            pe.wait_ge(S("ones_ready"), 1)
            pe.wait_ge(S("dt_ready"), 4)
            for a_, k in enumerate((2, 3, 5)):
                for c in range(2):
                    src = acum[:, c, :] if k == 3 else dts[:, k, c * P:(c + 1) * P]
                    o = (2 * a_ + c) * HEADS
                    tr(bank[0][:, o:o + HEADS], src, ident[0:HEADS, 0:HEADS])
            for f in range(ZT):
                for q in range(2):
                    mm(bank[1][q * HP:(q + 1) * HP, 17 * f:17 * f + 17],
                       bc(ident[0:HEADS, 2 * f + q:2 * f + q + 1], [HEADS, HP]), dts[:, 7, 0:17], start=True, stop=True)
            mm(bank[2][:, 0:HEADS], ones[0:HEADS, :], dts[:, 6, 0:HEADS], start=True, stop=True).then_inc(stage("dt_psum"), 1)
            for c in range(L1 * RING, RUN1):
                project(c, 2 * c, 0, 0)
            pe.wait_ge(S("bank_free"), 4 + 2 * RUN1)
            pe.wait_ge(S("dtok_ready"), 3)
            for half in range(2):
                if half:
                    pe.wait_ge(S("tail_ready"), 1)
                for f in range(12):
                    last = tr(bank[f // 4][0:11, (f % 4) * P:(f % 4 + 1) * P], proj[:, X0 + 12 * half + f, T - 11:T],
                              ident[:, :])
                last.then_inc(S("tail_psum"), 1)
            with pe.Fori(0, L2) as i:
                for j in range(RING):
                    c = RUN1 + j
                    project(c, 2 * c + 2 * RING * i, i, RING)
            for c in range(RUN1 + L2 * RING, N_PROJ):
                project(c, 2 * c, 0, 0)

            pe.wait_ge(S("consts_ready"), 3)
            pe.wait_ge(S("conv_done"), 13)
            pe.wait_ge(S("bank_free"), 4 + NT)
            pe.wait_ge(S("tail_ready"), 2)

            def ssd_prepare(it):
                c, gi = divmod(it, GROUPS)
                cols = slice(c * P, (c + 1) * P)
                if it:
                    pe.wait_ge(S("scores_ready"), it)
                    pe.wait_ge(S("btok_ready"), it)
                    if it > GROUPS:
                        pe.wait_ge(S("cexp_done"), it - GROUPS)
                for f in range(4):
                    tr(bank[0][:, f * P:(f + 1) * P], proj[:, X0 + 4 * gi + f, cols], ident[:, :])
                tr(bank[1][:, 0:P], proj[:, B0 + gi, cols], ident[:, :])
                mm(bank[1][:, P:2 * P], proj[:, B0 + gi, cols], proj[:, C0 + gi, cols], start=True, stop=True)
                for h in range(HPG):
                    hh = gi * HPG + h
                    last = mm(bank[2 + h // 4][:, (h % 4) * P:(h % 4 + 1) * P],
                              bc(ident[0:HEADS, hh:hh + 1], [HEADS, P]), acum[:, c, :], start=True, stop=True)
                last.then_inc(S("ssd_prep"), 1)

            def ssd_finish(it):
                c, gi = divmod(it, GROUPS)
                pe.wait_ge(S("scores_ready"), it + 1)
                pe.wait_ge(S("btok_ready"), it + 1)
                if it:
                    pe.wait_ge(S("y_done"), it)
                if c == 1:
                    pe.wait_ge(S("ctile_ready"), gi + 1)
                    pe.wait_ge(S("s0_ready"), GROUPS)
                for h in range(HPG):
                    q, f = h % 2, h // 2
                    out = bank[4][q * HP:(q + 1) * HP, f * P:(f + 1) * P]
                    last = mm(out, xdt[:, it % 2, h * HP:(h + 1) * HP], lmat[:, it % 2, h, :], start=True,
                              stop=(c == 0))
                    if c == 1:
                        hh = gi * HPG + h
                        last = mm(out, s0[:, hh * HP:(hh + 1) * HP], ctile[:, gi % 2, h, :], start=False, stop=True)
                last.then_inc(S("ssd_y"), 1)
                if 0 < it <= GROUPS:
                    pe.wait_ge(S("s0_ready"), it)
                if it > GROUPS:
                    pe.wait_ge(S("hT_ready"), it - GROUPS)
                mm(bank[5], btok[:, it % 2, :], xw[:, it % 2, :], start=True, stop=True).then_inc(S("ssd_state"), 1)

            def turn_state(gi):
                pe.wait_ge(S("hT_ready"), gi + 1)
                if gi:
                    pe.wait_ge(S("hout_ready"), gi)
                for f in range(4):
                    last = tr(bank[6][:, f * P:(f + 1) * P], hT[:, f * P:(f + 1) * P], ident[:, :])
                last.then_inc(S("hturn_psum"), 1)

            ssd_prepare(0)
            for it in range(2 * GROUPS):
                if it + 1 < 2 * GROUPS:
                    ssd_prepare(it + 1)
                if it > GROUPS:
                    turn_state(it - GROUPS - 1)
                ssd_finish(it)
            turn_state(GROUPS - 1)

            for b in range(TS):
                if b >= 2:
                    pe.wait_ge(S("hs_read"), b - 1)
                for k, first in enumerate((B0, C0)):
                    for gi in range(GROUPS):
                        last = mm(bank[2 * (b % 2) + k][:, gi * P:(gi + 1) * P],
                                  bc(proj[:, first + gi, TP + b:TP + b + 1], [P, P]), ident[:, :], start=True, stop=True)
                last.then_inc(S("bc_psum"), 1)
            pe.wait_ge(S("hs_read"), TS)
            for gi in range(GROUPS):
                pe.wait_ge(S("ysq_ready"), gi + 1)
                for f in range(4):
                    last = mm(bank[gi][:, 0:T], ones[:, :], ysq[:, 4 * gi + f, :], start=(f == 0), stop=(f == 3))
                last.then_inc(S("ss_psum"), 1)

            pe.wait_ge(*reached("norm_done"))
            for t in range(2):
                for f in range(12):
                    last = tr(bank[3 * t + f // 4][:, (f % 4) * P:(f % 4 + 1) * P], proj[:, K0 + f, t * P:(t + 1) * P],
                              ident[:, :])
                last.then_inc(S("kv_psum"), 1)
            pe.wait_ge(S("kvtok_ready"), 2)
            for f in range(QT):
                last = tr(bank[f // 4][0:TS, (f % 4) * P:(f % 4 + 1) * P], proj[:, Q0 + f, TP:T], ident[:, :])
            last.then_inc(stage("qkvs_psum"), 1)
            for h in range(NH):
                if h == 0:
                    pe.wait_ge(S("hout_ready"), GROUPS)
                if h >= 2:
                    pe.wait_ge(S("score_read"), h - 1)
                rows_ = slice(DH * (h % 2), DH * (h % 2) + DH)
                q, k = proj[rows_, Q0 + h // 2, :], proj[rows_, K0 + h // 2, :]
                b = bank[6 + h % 2]
                mm(b[:, 0:P], q[:, 0:P], k[:, 0:P], start=True, stop=True)
                mm(b[:, P:3 * P], q[:, P:2 * P], k[:, 0:2 * P], start=True, stop=True).then_inc(S("scores_psum"), 1)
            pe.wait_ge(S("qkvs_ready"), 2)
            for n in range(NH + 1):
                if n < NH:
                    hg, gi = divmod(n, 3)
                    h = gi * HG + hg
                    pe.wait_ge(S("pa_ready"), n + 1)
                    if n >= 2:
                        pe.wait_ge(S("pT_ready"), n - 1)
                    for blk in range(3):
                        last = tr(bank[n % 2][:, blk * P:(blk + 1) * P], pa[:, h, blk * P:(blk + 1) * P], ident[:, :])
                    last.then_inc(S("pturn_psum"), 1)
                if n:
                    m = n - 1
                    hg, gi = divmod(m, 3)
                    pe.wait_ge(S("pT_ready"), m + 1)
                    rows_ = slice(DH * (hg % 2), DH * (hg % 2) + DH)
                    cols = slice((hg // 2) * P, (hg // 2) * P + P)
                    vcol = slice((hg % 2) * DH, (hg % 2) * DH + DH)
                    vt = kvtok[:, :, 6 + 2 * gi + hg // 2, vcol]
                    mm(bank[2][rows_, cols], vt[:, 0, :], pT[:, m % 2, 0:P], start=(gi == 0), stop=(gi == 2))
                    mm(bank[3][rows_, cols], vt[:, 0, :], pT[:, m % 2, P:2 * P], start=(gi == 0), stop=False)
                    mm(bank[3][rows_, cols], vt[:, 1, :], pT[:, m % 2, 2 * P:3 * P], start=False,
                       stop=(gi == 2)).then_inc(S("pv_done"), 1)

            keys = [min(P, PAST // d) for _, d in DIL]
            for h in range(NH):
                gi = h // HG
                pe.wait_ge(S("qk_done"), gi + 1)
                if h == 2 * HG:
                    pe.wait_ge(S("oT_ready"), 1)
                last = tr(bank[gi][0:TS, (h % HG) * P:(h % HG) * P + keys[gi]], stok[0:keys[gi], h, :],
                          ident[0:keys[gi], 0:keys[gi]])
            last.then_inc(stage("sturn_psum"), 1)
            pe.wait_ge(*reached("sp_ready"))
            pe.wait_ge(S("oT_ready"), 2)
            for h in range(NH):
                n = keys[h // HG]
                last = tr(bank[3][0:n, TS * h:TS * h + TS], ss[:, h, 0:n], ident[0:TS, 0:TS])
            last.then_inc(stage("pj_psum"), 1)
            pe.wait_ge(*reached("selfo_ready"))
            for f in range(2):
                tr(bank[5][:, TS * f:TS * f + TS], selfo[:, f * P:(f + 1) * P], ident[0:TS, 0:TS])
            pe.wait_ge(S("pvs_ready"), 3)
            for b in range(TS):
                for f in range(2):
                    for gi in range(3):
                        last = mm(bank[4][:, TS * f + b:TS * f + b + 1], vsel[0:keys[gi], gi, b, f * P:(f + 1) * P],
                                  ones[0:keys[gi], 0:1], start=(gi == 0), stop=(gi == 2))
            last.then_inc(stage("so_psum"), 1)

            def raw_slices(n):
                raw_ready(pe, n)
                return wraw[:, n % RING, :].rearrange("p (a n) -> p a n", a=2)

            pe.wait_ge(S("oT_ready"), 3)
            for j in range(N_SSM):
                w = raw_slices(NATIVE0 + j)
                for m in range(KT):
                    for a_ in range(2):
                        last = mm(bank[m][:, 0:T], w[:, a_, m * P:(m + 1) * P], proj[:, 2 * j + a_, :],
                                  start=(j == 0 and a_ == 0), stop=(j == N_SSM - 1 and a_ == 1))
                    if j == N_SSM - 1:
                        last.then_inc(S("branch_a"), 1)
                if j < N_SSM - 1:
                    last.then_inc(S("native_used"), 1)
            w = raw_slices(NATIVE0 + N_SSM)
            for m in range(KT):
                pe.wait_ge(S("a_read"), m + 1)
                for a_ in range(2):
                    last = mm(bank[m][:, 0:T], w[:, a_, m * P:(m + 1) * P], oT[:, a_, :], start=(a_ == 0),
                              stop=(a_ == 1))
                last.then_inc(S("branch_b"), 1)
            pe.wait_ge(S("merge_done"), KT)
            for j in range(N_OUT):
                w = raw_slices(NATIVE0 + N_SSM + N_ATT + j)
                for t in range(3):
                    r = P if t < 2 else TS
                    for half in range(2):
                        for a_ in range(2):
                            last = mm(bank[2 * t + half][0:r, :], merged[:, 2 * j + a_, t * P:t * P + r],
                                      w[:, a_, 512 * half:512 * half + 512], start=(j == 0 and a_ == 0),
                                      stop=(j == N_OUT - 1 and a_ == 1))
                    if j == N_OUT - 1:
                        last.then_inc(S("mix_psum"), 1)
                if j < N_OUT - 1:
                    last.then_inc(S("native_used"), 1)

            pe.wait_ge(*reached("x1_ready"))
            for k in range(KT):
                for t in range(3):
                    r = P if t < 2 else TS
                    last = tr(bank[k][:, t * P:t * P + r], x1[0:r, t, k * P:(k + 1) * P], ident[0:r, 0:r])
                last.then_inc(S("x1T_psum"), 1)
            pe.wait_ge(S("x1T_ready"), KT)
            pe.wait_ge(S("router_in"), 48)
            for t in range(3):
                r = P if t < 2 else TS
                for k in range(KT):
                    last = mm(bank[0][0:r, t * NE:(t + 1) * NE], x1T[:, k, t * P:t * P + r], wr[:, k, :],
                              start=(k == 0), stop=(k == KT - 1))
            last.then_inc(stage("logits_psum"), 1)
            pe.wait_ge(*reached("mask_ready"))
            pe.wait_ge(S("ecol_ready"), 3)
            for t in range(4):
                for s in range(min(t, 2) + 1):
                    m = strict if s == t else ones
                    last = mm(bank[2][:, t * NE:(t + 1) * NE], m[:, :], mask[:, s, :], start=(s == 0),
                              stop=(s == min(t, 2)))
            last.then_inc(stage("rank_psum"), 1)
            pe.wait_ge(*reached("gm_ready"))
            for t in range(3):
                r = P if t < 2 else TS
                last = tr(bank[1][0:NE, t * P:t * P + r], gm[0:r, t, :], ident[0:r, 0:r])
            last.then_inc(stage("gmT_psum"), 1)
            pe.wait_ge(*reached("gmT_ready"))
            pe.wait_ge(*reached("table_ready"))

            nblk = pe.value_load(tab[0:1, MAX_BLK + 3:MAX_BLK + 4], min_val=NE, max_val=MAX_BLK)
            pe.wait_ge(*reached("x1l_done"))

            def gather(n):
                pe.wait_ge(S("oneh_ready"), n + 1)
                for half, src in enumerate((x1h, x1l)):
                    for k in range(KT):
                        for t in range(3):
                            last = mm(bank[6 + half][:, k * BLK:(k + 1) * BLK], src[:, t, k * P:(k + 1) * P],
                                      oneh[:, t, :], start=(t == 0), stop=(t == 2))
                last.then_inc(S("gath_done"), 1)

            def stream(n, rep, per, outs, stationary, first, final):
                hi, lo = pe_split(pe, n, rep, per)
                for i, (out, col) in enumerate(outs):
                    mm(out, stationary, hi[:, col:col + 512], start=first, stop=False)
                    last = mm(out, stationary, lo[:, col:col + 512], start=False, stop=final)
                return last

            def gate_up(b, rep, per):
                pe.wait_ge(S("xst_high"), b + 1)
                pe.wait_ge(S("xst_low"), b + 1)
                base = STEP0 if per else MOE0
                for k in range(GU_CH):
                    last = stream(base + k, rep, per, [(bank[i], 512 * i) for i in range(4)], xst[:, k, :], k == 0,
                                  k == GU_CH - 1)
                    last.then_inc(S("split_used"), 1)

            def down(n, base, rep, per):
                pe.wait_ge(S("hst_low"), n + 1)
                pe.wait_ge(S("low_read"), n + 1)
                for j in range(DN_CH):
                    hi, lo = pe_split(pe, base + j, rep, per)
                    for a_ in range(2):
                        k = 2 * j + a_
                        for half in range(2):
                            col = a_ * D + 512 * half
                            mm(bank[4 + half], hst[:, k, :], hi[:, col:col + 512], start=(k == 0), stop=False)
                            last = mm(bank[4 + half], hst[:, k, :], lo[:, col:col + 512], start=False,
                                      stop=(k == KT - 1))
                    last.then_inc(S("split_used"), 1)

            def turn_hidden(n):
                pe.wait_ge(S("hcopy_done"), n + 1)
                pe.wait_ge(S("xst_high"), n + 2)
                pe.wait_ge(S("xst_low"), n + 2)
                for f in range(2 * KT):
                    last = mm(bank[6 + f // KT][:, (f % KT) * BLK:(f % KT + 1) * BLK], hcopy[:, f * P:(f + 1) * P],
                              fold[:, :], start=True, stop=True)
                last.then_inc(S("ht_done"), 1)

            gather(0)
            gate_up(0, 0, 0)
            for t in range(3):
                r = P if t < 2 else TS
                if t:
                    pe.wait_ge(S("gb_read"), t)
                for half in range(2):
                    last = mm(bank[4 + half][0:r, :], gmT[:, t * P:t * P + r], bdn[:, 512 * half:512 * half + 512],
                              start=True, stop=True)
                last.then_inc(S("gb_psum"), 1)
            pe.wait_ge(S("gb_read"), 3)
            gather(1)
            turn_hidden(0)
            with pe.Fori(1, nblk) as b:
                pe.wait_ge(S("hcopy_done"), b)
                gate_up(b, b, 12)
                pe.wait_ge(S("ht_read"), b)
                gather(b + 1)
                down(b - 1, STEP0 + GU_CH, b, 12)
                turn_hidden(b)
            down(nblk - 1, STEP0, nblk, 12)


_INS = ["x_prompt", "x_sample", "state_ssm", "state_conv", "cache_kv_w128", "cache_kv_w512", "cache_kv_w2048", "w_in",
        "conv_w", "conv_b", "dt_bias", "a_log", "d_skip", "ssm_norm_g", "w_out_ssm", "w_out_attn", "w_out", "ln1_g",
        "ln1_b", "w_router", "b_router", "w_gate_up", "b_gate_up", "w_down", "b_down", "ln2_g", "ln2_b"]
_KV = [w for w, _ in DIL]
_OUTS = ([(1, TP, D), (TS, 1, D), (1, 1, HEADS, HP, NST), (1, 1, CW - 1, CONV_DIM)]
         + [(1, 1, w, 2, HG, DH) for w in _KV]
         + [(1, TS, HEADS, HP, NST), (1, TS, CW - 1, CONV_DIM)]
         + [(1, TS, w, 2, HG, DH) for w in _KV])


def kernel(**inputs):
    import concourse.bacc as _bacc
    from concourse.bass_utils import run_bass_kernel_spmd as _run

    nc = _bacc.Bacc("TRN2", target_bir_lowering=False, num_devices=1)
    arrays, args = {}, []
    for name in _INS:
        a = np.ascontiguousarray(inputs[name])
        arrays[f"in_{name}_dram"] = a
        args.append(nc.dram_tensor(f"in_{name}_dram", a.shape, mybir.dt.from_np(a.dtype), kind="ExternalInput").ap())
    for i, shape in enumerate(_OUTS):
        args.append(nc.dram_tensor(f"out_{i}_dram", shape, F32, kind="ExternalOutput").ap())
    build(nc, *args)
    r = _run(nc, [arrays], core_ids=[0])
    return tuple(r.results[0][f"out_{i}_dram"] for i in range(len(_OUTS)))
```
